# Optimizing a Trainium2 kernel written in Bass

```python
import jax, jax.numpy as jnp
from jax import lax
import numpy as np

D_MODEL = 2048
BATCH = 1
SEQ = 256
DEPTH = 1

POOL_WIDTH = D_MODEL // 2
POOL_WINDOWS = (2, 4, 8, 16)
N_POOL_GROUPS = len(POOL_WINDOWS)
POOL_GROUP = POOL_WIDTH // N_POOL_GROUPS
N_Q_HEADS = 16
N_KV_HEADS = 4
GROUP = N_Q_HEADS // N_KV_HEADS
HEAD_DIM = D_MODEL // N_Q_HEADS
NSA_WIDTH = N_Q_HEADS * HEAD_DIM
KV_WIDTH = N_KV_HEADS * HEAD_DIM
CMP_BLOCK = 32
CMP_STRIDE = 16
CMP_HIDDEN = 2 * HEAD_DIM
SEL_BLOCK = 64
N_SEL = 16
WINDOW = 512
Q_BLOCK = 128
ROPE_THETA = 10000.0
EPS = 1e-6
NEG = -1e30
FORCE = 1e6
N_BRANCHES = 2
IN_SPLITS = (POOL_WIDTH, POOL_WIDTH, NSA_WIDTH, KV_WIDTH, KV_WIDTH, KV_WIDTH, KV_WIDTH,
             KV_WIDTH, KV_WIDTH, NSA_WIDTH, 3 * N_Q_HEADS)
D_IN = sum(IN_SPLITS)


def rmsnorm(x, w):
    xf = x.astype(jnp.float32)
    y = xf * lax.rsqrt(jnp.mean(xf * xf, axis=-1, keepdims=True) + EPS)
    return (y * w.astype(jnp.float32)).astype(x.dtype)

def rope(x, pos):
    half = HEAD_DIM // 2
    inv = ROPE_THETA ** (-jnp.arange(half, dtype=jnp.float32) / half)
    ang = pos.astype(jnp.float32)[:, None] * inv[None, :]
    cos = jnp.cos(ang)[None, :, None, :]
    sin = jnp.sin(ang)[None, :, None, :]
    xf = x.astype(jnp.float32)
    x1, x2 = xf[..., :half], xf[..., half:]
    return jnp.concatenate([x1 * cos - x2 * sin, x2 * cos + x1 * sin], axis=-1).astype(x.dtype)

def pool_mixer(u, mix, scale):
    b, s, _ = u.shape
    ug = u.reshape(b, s, N_POOL_GROUPS, POOL_GROUP)
    uf = ug.astype(jnp.float32)
    c = jnp.pad(jnp.cumsum(uf, axis=1), ((0, 0), (1, 0), (0, 0), (0, 0)))
    t = np.arange(s)
    win = np.array(POOL_WINDOWS)
    lo = np.maximum(t[:, None] + 1 - win[None, :], 0)
    cnt = jnp.asarray(np.minimum(t[:, None] + 1, win[None, :]).astype(np.float32))
    c_lo = c[:, lo, np.arange(N_POOL_GROUPS)[None, :]]
    mean = (c[:, 1:] - c_lo) / cnt[None, :, :, None]
    pooled = (mean - uf).astype(u.dtype)
    z = jnp.einsum("bsgc,gcd->bsgd", pooled, mix).reshape(b, s, POOL_WIDTH)
    return z * scale

def compress(kraw, pe, w1, w2):
    s = kraw.shape[1]
    n_cmp = (s - CMP_BLOCK) // CMP_STRIDE + 1
    idx = np.arange(n_cmp)[:, None] * CMP_STRIDE + np.arange(CMP_BLOCK)[None, :]
    kb = kraw[:, idx] + pe[None, None, :, None, :]
    hdn = jax.nn.silu(jnp.einsum("bnlhd,ldf->bnhf", kb, w1))
    return jnp.einsum("bnhf,fe->bnhe", hdn, w2)

def nsa_attention(q, kc, vc, ks, vs, kw, vw, gates):
    b, s = q.shape[0], q.shape[1]
    n_cmp = kc.shape[1]
    n_blk = s // SEL_BLOCK
    n_sel = min(N_SEL, n_blk)
    scale = HEAD_DIM ** -0.5
    cmp_end = jnp.arange(n_cmp) * CMP_STRIDE + CMP_BLOCK - 1
    ratio = SEL_BLOCK // CMP_STRIDE
    sub = CMP_BLOCK // CMP_STRIDE
    sel_idx = (np.arange(n_blk)[:, None, None] * ratio + np.arange(ratio)[None, :, None]
               - np.arange(sub)[None, None, :]).reshape(n_blk, ratio * sub)
    sel_valid = jnp.asarray((sel_idx >= 0) & (sel_idx < n_cmp))
    sel_idx = np.clip(sel_idx, 0, n_cmp - 1)
    ks_blk = ks.reshape(b, n_blk, SEL_BLOCK, N_KV_HEADS, HEAD_DIM).transpose(0, 3, 1, 2, 4)
    vs_blk = vs.reshape(b, n_blk, SEL_BLOCK, N_KV_HEADS, HEAD_DIM).transpose(0, 3, 1, 2, 4)
    kw_pad = jnp.pad(kw, ((0, 0), (WINDOW, 0), (0, 0), (0, 0)))
    vw_pad = jnp.pad(vw, ((0, 0), (WINDOW, 0), (0, 0), (0, 0)))
    gather = jax.vmap(jax.vmap(lambda kt, ix: kt[ix]))
    jblk = jnp.arange(n_blk)

    def block(i):
        s0 = i * Q_BLOCK
        qb = lax.dynamic_slice_in_dim(q, s0, Q_BLOCK, axis=1)
        gb = lax.dynamic_slice_in_dim(gates, s0, Q_BLOCK, axis=1)
        tpos = s0 + jnp.arange(Q_BLOCK)
        sc = jnp.einsum("bqhgd,bnhd->bhgqn", qb, kc, preferred_element_type=jnp.float32) * scale
        cvalid = cmp_end[None, :] <= tpos[:, None]
        p_c = jnp.where(cvalid, jax.nn.softmax(jnp.where(cvalid, sc, NEG), axis=-1), 0.0)
        o_c = jnp.einsum("bhgqn,bnhe->bqhge", p_c.astype(vc.dtype), vc)
        imp_c = p_c.sum(axis=2)
        imp = jnp.where(sel_valid, imp_c[..., sel_idx], 0.0).sum(-1)
        jt = (tpos // SEL_BLOCK)[:, None]
        forced = (jblk[None, :] == 0) | (jblk[None, :] == jt) | (jblk[None, :] == jt - 1)
        imp = jnp.where(forced, FORCE, imp)
        imp = jnp.where(jblk[None, :] > jt, NEG, imp)
        _, top = lax.top_k(imp, n_sel)
        kg = gather(ks_blk, top)
        vg = gather(vs_blk, top)
        kpos = top[..., None] * SEL_BLOCK + jnp.arange(SEL_BLOCK)
        svalid = kpos <= tpos[None, None, :, None, None]
        ss = jnp.einsum("bqhgd,bhqnld->bhgqnl", qb, kg, preferred_element_type=jnp.float32) * scale
        ss = jnp.where(svalid[:, :, None], ss, NEG)
        p_s = jax.nn.softmax(ss.reshape(ss.shape[:4] + (-1,)), axis=-1).reshape(ss.shape)
        o_s = jnp.einsum("bhgqnl,bhqnle->bqhge", p_s.astype(vg.dtype), vg)
        kwb = lax.dynamic_slice_in_dim(kw_pad, s0, WINDOW + Q_BLOCK, axis=1)
        vwb = lax.dynamic_slice_in_dim(vw_pad, s0, WINDOW + Q_BLOCK, axis=1)
        wpos = s0 - WINDOW + jnp.arange(WINDOW + Q_BLOCK)
        diff = tpos[:, None] - wpos[None, :]
        wvalid = (diff >= 0) & (diff < WINDOW) & (wpos[None, :] >= 0)
        sw = jnp.einsum("bqhgd,bkhd->bhgqk", qb, kwb, preferred_element_type=jnp.float32) * scale
        p_w = jax.nn.softmax(jnp.where(wvalid, sw, NEG), axis=-1)
        o_w = jnp.einsum("bhgqk,bkhe->bqhge", p_w.astype(vwb.dtype), vwb)
        return gb[..., 0:1] * o_c + gb[..., 1:2] * o_s + gb[..., 2:3] * o_w

    out = lax.map(block, jnp.arange(s // Q_BLOCK))
    return out.transpose(1, 0, 2, 3, 4, 5).reshape(b, s, NSA_WIDTH)

def first_inputs(seed: int = 0) -> dict:
    key = jax.random.key(seed)
    ks = jax.random.split(key, 20)
    f32 = jnp.float32
    nrm = lambda k, shape, fan: jax.random.normal(k, shape, f32) * (fan ** -0.5)
    L = DEPTH
    return {
        "x": jax.random.normal(ks[0], (BATCH, SEQ, D_MODEL), f32),
        "norm_w": 1.0 + 0.05 * jax.random.normal(ks[1], (L, D_MODEL), f32),
        "w_in": nrm(ks[2], (L, D_MODEL, D_IN), D_MODEL),
        "pool_mix": nrm(ks[3], (L, N_POOL_GROUPS, POOL_GROUP, POOL_GROUP), POOL_GROUP),
        "pool_scale": 1.0 + 0.1 * jax.random.normal(ks[4], (L, POOL_WIDTH), f32),
        "cmp_pe_k": 0.1 * jax.random.normal(ks[5], (L, CMP_BLOCK, HEAD_DIM), f32),
        "cmp_w1_k": nrm(ks[6], (L, CMP_BLOCK, HEAD_DIM, CMP_HIDDEN), CMP_BLOCK * HEAD_DIM),
        "cmp_w2_k": nrm(ks[7], (L, CMP_HIDDEN, HEAD_DIM), CMP_HIDDEN),
        "cmp_pe_v": 0.1 * jax.random.normal(ks[8], (L, CMP_BLOCK, HEAD_DIM), f32),
        "cmp_w1_v": nrm(ks[9], (L, CMP_BLOCK, HEAD_DIM, CMP_HIDDEN), CMP_BLOCK * HEAD_DIM),
        "cmp_w2_v": nrm(ks[10], (L, CMP_HIDDEN, HEAD_DIM), CMP_HIDDEN),
        "w_pool_out": nrm(ks[11], (L, POOL_WIDTH, D_MODEL), POOL_WIDTH),
        "w_nsa_out": nrm(ks[12], (L, NSA_WIDTH, D_MODEL), NSA_WIDTH),
        "w_merge": nrm(ks[13], (L, D_MODEL, N_BRANCHES * D_MODEL), D_MODEL),
        "b_merge": 0.01 * jax.random.normal(ks[14], (L, N_BRANCHES * D_MODEL), f32),
        "w_out": nrm(ks[15], (L, D_MODEL, D_MODEL), D_MODEL),
        "final_norm_w": 1.0 + 0.05 * jax.random.normal(ks[16], (D_MODEL,), f32),
    }

def first_block(x, norm_w, w_in, pool_mix, pool_scale, cmp_pe_k, cmp_w1_k, cmp_w2_k,
              cmp_pe_v, cmp_w1_v, cmp_w2_v, w_pool_out, w_nsa_out, w_merge, b_merge,
              w_out, final_norm_w):
    b, s, _ = x.shape
    pos = jnp.arange(s)
    n_cmp = (s - CMP_BLOCK) // CMP_STRIDE + 1
    cmp_pos = jnp.arange(n_cmp) * CMP_STRIDE + CMP_BLOCK - 1
    split_at = np.cumsum(IN_SPLITS)[:-1].tolist()
    for layer in range(DEPTH):
        h = rmsnorm(x, norm_w[layer])
        proj = h @ w_in[layer]
        (u_pool, g_pool, q, kc_raw, vc_raw, k_sel, v_sel, k_win, v_win,
         g_nsa, g_br) = jnp.split(proj, split_at, axis=-1)
        y_pool = pool_mixer(u_pool, pool_mix[layer], pool_scale[layer]) * jax.nn.silu(g_pool)
        y_a = y_pool @ w_pool_out[layer]
        heads = lambda t, n: t.reshape(b, s, n, HEAD_DIM)
        qh = rope(heads(q, N_Q_HEADS), pos).reshape(b, s, N_KV_HEADS, GROUP, HEAD_DIM)
        kc = rope(compress(heads(kc_raw, N_KV_HEADS), cmp_pe_k[layer], cmp_w1_k[layer],
                           cmp_w2_k[layer]), cmp_pos)
        vc = compress(heads(vc_raw, N_KV_HEADS), cmp_pe_v[layer], cmp_w1_v[layer], cmp_w2_v[layer])
        ksh = rope(heads(k_sel, N_KV_HEADS), pos)
        kwh = rope(heads(k_win, N_KV_HEADS), pos)
        gates = jax.nn.sigmoid(g_br).reshape(b, s, N_KV_HEADS, GROUP, 3)
        o_nsa = nsa_attention(qh, kc, vc, ksh, heads(v_sel, N_KV_HEADS), kwh,
                              heads(v_win, N_KV_HEADS), gates)
        y_b = (o_nsa * jax.nn.silu(g_nsa)) @ w_nsa_out[layer]
        gm = jax.nn.sigmoid(h @ w_merge[layer] + b_merge[layer]).reshape(b, s, N_BRANCHES, D_MODEL)
        merged = gm[:, :, 0] * y_a + gm[:, :, 1] * y_b
        x = x + merged @ w_out[layer]
    return rmsnorm(x, final_norm_w)


HEAD_DIM_2 = 128
N_HEADS_A = D_MODEL // 256
N_KV_A = max(1, N_HEADS_A // 4)
N_HEADS_B = D_MODEL // 256
GRID_W = 64
NA_ROWS = 8
NA_COLS = 16
ROPE_AXIS_DIM = HEAD_DIM_2 // 2
D_FF = -(-(8 * D_MODEL) // (3 * 256)) * 256
NORM_EPS = 1e-6
IN_SPLITS_2 = (
    N_HEADS_A * HEAD_DIM_2,
    N_KV_A * HEAD_DIM_2,
    N_KV_A * HEAD_DIM_2,
    N_HEADS_B * HEAD_DIM_2,
    N_HEADS_B * HEAD_DIM_2,
    N_HEADS_B * HEAD_DIM_2,
    D_MODEL,
    D_MODEL,
)
D_IN_2 = sum(IN_SPLITS_2)


def rms_norm(x, w):
    xf = x.astype(jnp.float32)
    y = xf * lax.rsqrt(jnp.mean(xf * xf, axis=-1, keepdims=True) + NORM_EPS)
    return (y * w.astype(jnp.float32)).astype(x.dtype)

def axial_rope_tables(S):
    t = jnp.arange(S, dtype=jnp.int32)
    row = (t // GRID_W).astype(jnp.float32)
    col = (t % GRID_W).astype(jnp.float32)
    inv = ROPE_THETA ** (-jnp.arange(0, ROPE_AXIS_DIM, 2, dtype=jnp.float32) / ROPE_AXIS_DIM)
    ang = jnp.concatenate([row[:, None] * inv[None], col[:, None] * inv[None]], axis=-1)
    return jnp.cos(ang), jnp.sin(ang)

def apply_rope(x, cos, sin):
    xf = x.astype(jnp.float32).reshape(*x.shape[:-1], HEAD_DIM_2 // 2, 2)
    x0, x1 = xf[..., 0], xf[..., 1]
    c = cos[None, :, None, :]
    s = sin[None, :, None, :]
    out = jnp.stack([x0 * c - x1 * s, x0 * s + x1 * c], axis=-1)
    return out.reshape(x.shape).astype(x.dtype)

def global_gqa(q, k, v):
    B, S, HQ, hd = q.shape
    KVH = k.shape[2]
    G = HQ // KVH
    nb = S // Q_BLOCK
    scale = hd ** -0.5
    qb = q.reshape(B, nb, Q_BLOCK, KVH, G, hd).transpose(1, 0, 2, 3, 4, 5)

    def one_block(qblk):
        s = jnp.einsum('bqkgd,bskd->bkgqs', qblk, k).astype(jnp.float32) * scale
        p = jax.nn.softmax(s, axis=-1).astype(v.dtype)
        return jnp.einsum('bkgqs,bskd->bqkgd', p, v)

    o = lax.map(one_block, qb)
    return o.transpose(1, 0, 2, 3, 4, 5).reshape(B, S, HQ * hd)

def neighbourhood_attention(q, k, v, rpb):
    B, S, H, hd = q.shape
    rows = S // GRID_W
    kr = min(NA_ROWS, rows)
    nk = kr * NA_COLS
    nb = S // Q_BLOCK
    scale = hd ** -0.5
    t = jnp.arange(S, dtype=jnp.int32)
    r = t // GRID_W
    col = t % GRID_W
    rs = jnp.clip(r - kr // 2, 0, rows - kr)
    cs = jnp.clip(col - NA_COLS // 2, 0, GRID_W - NA_COLS)
    key_r = rs[:, None, None] + jnp.arange(kr, dtype=jnp.int32)[None, :, None]
    key_c = cs[:, None, None] + jnp.arange(NA_COLS, dtype=jnp.int32)[None, None, :]
    shape3 = (S, kr, NA_COLS)
    idx = (key_r * GRID_W + key_c).reshape(nb, Q_BLOCK, nk)
    rel_r = jnp.broadcast_to(key_r - r[:, None, None] + (NA_ROWS - 1), shape3).reshape(nb, Q_BLOCK, nk)
    rel_c = jnp.broadcast_to(key_c - col[:, None, None] + (NA_COLS - 1), shape3).reshape(nb, Q_BLOCK, nk)
    qb = q.reshape(B, nb, Q_BLOCK, H, hd).transpose(1, 0, 2, 3, 4)

    def one_block(args):
        qblk, ib, rr, rc = args
        kb = k[:, ib]
        vb = v[:, ib]
        bias = rpb[:, rr, rc].astype(jnp.float32)
        s = jnp.einsum('bqhd,bqnhd->bhqn', qblk, kb).astype(jnp.float32) * scale + bias[None]
        p = jax.nn.softmax(s, axis=-1).astype(v.dtype)
        return jnp.einsum('bhqn,bqnhd->bqhd', p, vb)

    o = lax.map(one_block, (qb, idx, rel_r, rel_c))
    return o.transpose(1, 0, 2, 3, 4).reshape(B, S, H * hd)

def second_inputs(seed: int = 0) -> dict:
    key = jax.random.key(seed)
    ks = jax.random.split(key, 20)
    f32 = jnp.float32
    D = D_MODEL

    def w(k, shape, fan_in):
        return jax.random.normal(k, shape, f32) * (fan_in ** -0.5)

    def gain(k, shape):
        return 1.0 + 0.05 * jax.random.normal(k, shape, f32)

    return {
        "x": jax.random.normal(ks[0], (BATCH, SEQ, D), f32),
        "c": jax.random.normal(ks[1], (BATCH, D), f32),
        "w_ada": w(ks[2], (DEPTH, D, 6 * D), D) * 0.5,
        "b_ada": 0.02 * jax.random.normal(ks[3], (DEPTH, 6 * D), f32),
        "norm1_w": gain(ks[4], (DEPTH, D)),
        "w_in": w(ks[5], (DEPTH, D, D_IN_2), D),
        "q_norm_w": gain(ks[6], (DEPTH, HEAD_DIM_2)),
        "k_norm_w": gain(ks[7], (DEPTH, HEAD_DIM_2)),
        "nat_rpb": 0.1 * jax.random.normal(ks[8], (DEPTH, N_HEADS_B, 2 * NA_ROWS - 1, 2 * NA_COLS - 1), f32),
        "w_oa": w(ks[9], (DEPTH, N_HEADS_A * HEAD_DIM_2, D), N_HEADS_A * HEAD_DIM_2),
        "w_ob": w(ks[10], (DEPTH, N_HEADS_B * HEAD_DIM_2, D), N_HEADS_B * HEAD_DIM_2),
        "w_out": w(ks[11], (DEPTH, D, D), D),
        "norm2_w": gain(ks[12], (DEPTH, D)),
        "w_ffn_gate": w(ks[13], (DEPTH, D, D_FF), D),
        "w_ffn_up": w(ks[14], (DEPTH, D, D_FF), D),
        "w_ffn_down": w(ks[15], (DEPTH, D_FF, D), D_FF),
        "final_w": gain(ks[16], (D,)),
    }

def second_block(x, c, w_ada, b_ada, norm1_w, w_in, q_norm_w, k_norm_w, nat_rpb,
              w_oa, w_ob, w_out, norm2_w, w_ffn_gate, w_ffn_up, w_ffn_down, final_w):
    B, S, D = x.shape
    cos, sin = axial_rope_tables(S)
    offs = np.cumsum(IN_SPLITS_2)[:-1].tolist()
    c_act = jax.nn.silu(c)
    for l in range(DEPTH):
        mod = c_act @ w_ada[l] + b_ada[l]
        sh1, sc1, g1, sh2, sc2, g2 = [m[:, None, :] for m in jnp.split(mod, 6, axis=-1)]

        h = rms_norm(x, norm1_w[l]) * (1.0 + sc1) + sh1
        proj = h @ w_in[l]
        qa, ka, va, qb, kb, vb, ga, gb = jnp.split(proj, offs, axis=-1)
        qa = qa.reshape(B, S, N_HEADS_A, HEAD_DIM_2)
        ka = ka.reshape(B, S, N_KV_A, HEAD_DIM_2)
        va = va.reshape(B, S, N_KV_A, HEAD_DIM_2)
        qa = apply_rope(rms_norm(qa, q_norm_w[l]), cos, sin)
        ka = apply_rope(rms_norm(ka, k_norm_w[l]), cos, sin)
        ya = global_gqa(qa, ka, va)
        yb = neighbourhood_attention(
            qb.reshape(B, S, N_HEADS_B, HEAD_DIM_2),
            kb.reshape(B, S, N_HEADS_B, HEAD_DIM_2),
            vb.reshape(B, S, N_HEADS_B, HEAD_DIM_2),
            nat_rpb[l])
        merged = jax.nn.sigmoid(ga) * (ya @ w_oa[l]) + jax.nn.sigmoid(gb) * (yb @ w_ob[l])
        x = x + g1 * (merged @ w_out[l])

        h2 = rms_norm(x, norm2_w[l]) * (1.0 + sc2) + sh2
        ff = (jax.nn.silu(h2 @ w_ffn_gate[l]) * (h2 @ w_ffn_up[l])) @ w_ffn_down[l]
        x = x + g2 * ff
    return rms_norm(x, final_w)


def setup_inputs(seed=0):
    out = dict(first_inputs(seed))
    for name, value in second_inputs(seed + 1).items():
        if name != "x":
            out[name + "_2"] = value
    return out


def reference(
    x, norm_w, w_in, pool_mix, pool_scale, cmp_pe_k, cmp_w1_k, cmp_w2_k, cmp_pe_v, cmp_w1_v,
    cmp_w2_v, w_pool_out, w_nsa_out, w_merge, b_merge, w_out, final_norm_w, c_2, w_ada_2,
    b_ada_2, norm1_w_2, w_in_2, q_norm_w_2, k_norm_w_2, nat_rpb_2, w_oa_2, w_ob_2, w_out_2,
    norm2_w_2, w_ffn_gate_2, w_ffn_up_2, w_ffn_down_2, final_w_2,
):
    x = first_block(
        x, norm_w, w_in, pool_mix, pool_scale, cmp_pe_k, cmp_w1_k, cmp_w2_k, cmp_pe_v, cmp_w1_v,
        cmp_w2_v, w_pool_out, w_nsa_out, w_merge, b_merge, w_out, final_norm_w,
    )
    return second_block(
        x, c_2, w_ada_2, b_ada_2, norm1_w_2, w_in_2, q_norm_w_2, k_norm_w_2, nat_rpb_2, w_oa_2,
        w_ob_2, w_out_2, norm2_w_2, w_ffn_gate_2, w_ffn_up_2, w_ffn_down_2, final_w_2,
    )


_drawn_inputs = setup_inputs


def setup_inputs(seed=0):
    import zlib

    import numpy as np

    out = dict(_drawn_inputs(seed))
    spreads = {}
    factors = {'cmp_pe_k': 8.0,
     'cmp_w1_k': 3.286,
     'cmp_w2_k': 3.148,
     'cmp_pe_v': 7.384,
     'b_merge': 8.0,
     'b_ada_2': 3.214,
     'norm1_w_2': 8.0,
     'q_norm_w_2': 8.0,
     'k_norm_w_2': 8.0,
     'nat_rpb_2': 8.0,
     'norm2_w_2': 3.652}
    for name, (base, spread) in spreads.items():
        noise = np.random.default_rng([zlib.crc32(name.encode()), seed]).standard_normal(out[name].shape)
        drawn = base * np.exp(spread * noise) if base else spread * noise
        out[name] = __import__('jax').numpy.asarray(drawn.astype(out[name].dtype))
    for name, factor in factors.items():
        out[name] = (out[name] * factor).astype(out[name].dtype)
    return out
```

```python
from contextlib import ExitStack, contextmanager

import numpy as np

import concourse.bass as bass
from concourse import mybir

ALU = mybir.AluOpType
ACT = mybir.ActivationFunctionType
AX = mybir.AxisListType
F32 = mybir.dt.float32
F32R = mybir.dt.float32r

P = 128
S = 256
TB = S // P
D = 2048
KT = D // P
NC = 512
TW = 1024
RING = 4
ADA_RING = 3
N_CONSTS = 13
EPS = 1e-6
NEG = -1e30
HD = 128
HALF = HD // 2
SCALE = HD ** -0.5
POOL_W = 1024
WINDOWS = (2, 4, 8, 16)
POOL_G = POOL_W // len(WINDOWS)
NQ, NKV = 16, 4
CMP_BLOCK, CMP_STRIDE = 32, 16
N_CMP = (S - CMP_BLOCK) // CMP_STRIDE + 1
CMP_ROWS = NKV * N_CMP
CMP_H = 2 * HD
GRID_W, NA_ROWS, NA_COLS = 64, 8, 16
ROWS = S // GRID_W
D_FF = -(-(8 * D) // (3 * 256)) * 256
FC = D_FF // NC
N_ADA = 6 * D // P
assert S // 64 <= 16 and S <= 512 and ROWS <= NA_ROWS

C_IN = 18
C_IN2 = 9
T_K = D // 256
T_H = T_K // 2
T_Q = T_K // 4
PHASES = [
    ("proj", C_IN * T_K), ("gbr", 1), ("cmp_k", 8), ("cmp_v", 8), ("pool_out", 4 * T_H),
    ("merge_a", 4 * T_K), ("merge_b", 4 * 2 * T_K), ("out1", 4 * T_K),
    ("proj2", C_IN2 * T_K), ("merge2", 4 * (2 * T_K + 2 * T_H)), ("out2", 4 * T_K),
    ("ff_first", 2 * T_K), ("ff", (FC - 1) * (2 * T_K + 4 * T_Q)), ("ff_last", 4 * T_Q),
]
T0, N_TILES = {}, 0
for _name, _n in PHASES:
    T0[_name] = N_TILES
    N_TILES += _n
CHUNKS = [
    ("proj", C_IN), ("gbr", 1), ("cmp_k", 1), ("cmp_v", 1), ("pool_out", 4), ("merge_a", 4),
    ("merge_b", 8), ("out1", 4), ("proj2", C_IN2), ("merge2", 16), ("out2", 4),
    ("ff_first", 2), ("ff", 6 * (FC - 1)), ("ff_last", 4),
]
G0, _g = {}, 0
for _name, _n in CHUNKS:
    G0[_name] = _g
    _g += _n
ADA_PER_CHUNK = {"proj": 6, "merge_a": 6, "merge_b": 6, "out1": 3}
ADA0, _a = {}, 0
for _name, _c in (("proj", C_IN), ("merge_a", 4), ("merge_b", 8), ("out1", 4)):
    ADA0[_name] = _a
    _a += _c * ADA_PER_CHUNK[_name]
assert _a == 2 * N_ADA, _a


class At:

    def __init__(self, base, per=0, i=None):
        self.base, self.per, self.i = base, per, i

    def __add__(self, k):
        return At(self.base + k, self.per, self.i)

    @property
    def n(self):
        return self.base if self.i is None else self.per * self.i + self.base

    def slot(self, ring):
        assert self.per % ring == 0
        return self.base % ring

    def lap(self, ring, scale):
        c = (self.base // ring + 1) * scale
        return c if self.i is None else (self.per // ring * scale) * self.i + c


class Count:

    def __init__(self, sem):
        self.sem, self.n, self.local = sem, 0, 0

    def on(self, ins):
        ins.then_inc(self.sem, 1)
        self.n = self.n + 1
        self.local += 1


@contextmanager
def turns(eng, times, count, per):
    start = count.n
    with eng.Fori(0, times) as i:
        count.n, count.local = per * i + start, 0
        yield i
    assert count.local == per, (count.local, per)
    count.n = start + per * times


def build(nc, t):
    ctx = ExitStack()
    with ctx:
        K = 1024
        top = [ctx.enter_context(nc.sbuf_tensor("arena", [P, 212800 // 4], F32))]
        base = nc.sbuf_base - 212800
        base = (base + 31) // 32 * 32
        limit = base + 212700

        def at(name, off, shape, dt=F32):
            size = int(np.prod(shape[1:])) * 4
            assert base + off + size <= limit, (name, off + size)
            return nc.alloc_sbuf_tensor_at(name, shape, dt, offset=base + off)

        def sem(name):
            return ctx.enter_context(nc.semaphore(name))

        raw = at("raw", 0, [P, RING, TW])
        w_hi = at("w_hi", 16 * K, [P, RING, TW], F32R)
        w_lo = at("w_lo", 32 * K, [P, RING, TW], F32R)
        a_hi = at("a_hi", 48 * K, [P, KT, S], F32R)
        a_lo = at("a_lo", 64 * K, [P, KT, S], F32R)
        o = [80 * K]

        def const(name, shape):
            r = at(name, o[0], shape)
            o[0] += (int(np.prod(shape[1:])) * 4 + 31) // 32 * 32
            return r

        ident = const("ident", [P, P])
        trig1 = const("trig1", [P, 2, TB, HALF])
        trig2 = const("trig2", [P, 2, TB, HALF])
        trigc = const("trigc", [N_CMP, 2, HALF])
        causal = const("causal", [P, P])
        cmask = const("cmask", [P, TB, N_CMP])
        cvalid = const("cvalid", [P, TB, N_CMP])
        n1T = const("n1T", [P, KT])
        n1T_2 = const("n1T_2", [P, KT])
        n2T_2 = const("n2T_2", [P, KT])
        peT = const("peT", [P, 2, CMP_BLOCK])
        b_adaT = const("b_adaT", [P, N_ADA])
        qkn = const("qkn", [P, 2, HD])
        mod_part = const("mod_part", [P, 12])
        mod2 = const("mod2", [P, 2 * N_ADA])
        mod = const("mod", [P, N_ADA])
        scale1 = const("scale1", [P, KT])
        scale2 = const("scale2", [P, KT])
        ssq = const("ssq", [P, TB])
        rstd = const("rstd", [P, TB])
        gates = const("gates", [P, TB, 3 * NQ])
        hss = const("hss", [P, TB, 5])
        nmax = const("nmax", [P, 8])
        nms = const("nms", [P, 8])
        den = const("den", [P, 8])
        coef = const("coef", [P, 8])
        cmx = const("cmx", [P, 4])
        cden = const("cden", [P, 4])
        pc = const("pc", [P, 4, N_CMP])
        kcT = const("kcT", [P, CMP_ROWS])
        assert o[0] <= 89 * K, o[0]

        ADA = 89 * K
        ada = at("ada", ADA, [P, ADA_RING, TW])
        cb = at("cb", ADA + 12 * K, [P, D])
        kT2 = at("kT2", ADA, [P, 4, S])
        kr2 = at("kr2", ADA + 4 * K, [P, TB, HD])
        na_bias = at("na_bias", ADA + 8 * K, [P, 4, S])
        g12 = at("g12", ADA, [P, 2, 4, NC])
        R = ADA + 20 * K
        proj = at("proj", R, [P, C_IN, TB, NC])
        y_hi = at("y_hi", R + 24 * K, [P, 4, 4, S], F32R)
        y_lo = at("y_lo", R + 56 * K, [P, 4, 4, S], F32R)
        yp_hi = at("yp_hi", R, [P, 8, S], F32R)
        yp_lo = at("yp_lo", R + 8 * K, [P, 8, S], F32R)
        scale_b = at("scale_b", R + 16 * K, [P, 2, NC])
        b_b = at("b_b", R, [P, 8, NC])
        x1 = at("x1", R + 40 * K, [P, 4, TB, NC])
        ya_hi = at("ya_hi", R, [P, 2, 4, S], F32R)
        yb_hi = at("yb_hi", R + 12 * K, [P, 2, 4, S], F32R)
        ya_lo = at("ya_lo", R + 56 * K, [P, 2, 4, S], F32R)
        yb_lo = at("yb_lo", R + 64 * K, [P, 2, 4, S], F32R)
        f_hi = at("f_hi", R, [P, 4, S], F32R)
        f_lo = at("f_lo", R + 4 * K, [P, 4, S], F32R)
        acc = at("acc", R + 8 * K, [P, 4, TB, NC])
        f_silu = at("f_silu", R + 24 * K, [P, TB, NC])
        f_act = at("f_act", R + 28 * K, [P, TB, NC])
        final_b = at("final_b", R + 32 * K, [P, 4, NC])
        SC = R + 72 * K
        xn = at("xn", SC, [P, 4, TB, NC])
        xt = at("xt", SC + 16 * K, [P, 2, NC])
        x0 = at("x0", R, [P, 4, TB, NC])
        ckT = at("ckT", SC, [P, 2, NKV, S])
        kbf = at("kbf", SC + 8 * K, [P, CMP_BLOCK, CMP_ROWS])
        kb_hi = at("kb_hi", SC + 16 * K, [P, CMP_BLOCK, CMP_ROWS], F32R)
        kb_lo = at("kb_lo", R, [P, CMP_BLOCK, CMP_ROWS], F32R)
        w2 = at("w2", SC + 8 * K, [P, 2, 2, HD])
        kcr = at("kcr", SC + 10 * K, [N_CMP, NKV, HD])
        kct = at("kct", SC + 12 * K, [N_CMP, 4, NKV, HALF])
        hdn = at("hdn", SC + 24 * K, [CMP_ROWS, CMP_H])
        hdnT = at("hdnT", SC + 25 * K, [P, 2, 2, CMP_ROWS])
        prob = at("prob", SC, [P, 8, S])
        rt = at("rt", SC, [P, 4, TB, 4, HALF])
        pt = at("pt", SC + 8 * K, [P, 2, NC])
        sg = at("sg", SC + 8 * K, [P, TB, NC])
        qT = at("qT", SC + 12 * K, [P, 4, S])
        gT = at("gT", SC + 16 * K, [P, 4, S])
        qr = at("qr", SC + 20 * K, [P, TB, 4, HD])
        pcT = at("pcT", SC + 20 * K, [N_CMP, NC])
        ot = at("ot", SC + 22 * K, [P, NC])
        vg = at("vg", SC + 24 * K, [P, TB, 2, HD])
        vcg = at("vcg", SC + 26 * K, [N_CMP, HD])
        kT1 = at("kT1", R, [P, 4, S])
        kr1 = at("kr1", R + 4 * K, [P, TB, 2, HD])
        vc = at("vc", R + 6 * K, [N_CMP, NKV, HD])
        band = at("band", SC, [P, 4, TB, S])
        mix = at("mix", SC + 8 * K, [P, 4, 2, POOL_G])
        poT = at("poT", SC + 16 * K, [P, 8, S])
        ya = at("ya", SC, [P, 4, TB, NC])
        ga = at("ga", SC + 16 * K, [P, TB, NC])
        gb = at("gb", SC + 20 * K, [P, TB, NC])

        ps = ctx.enter_context(nc.psum_tensor("ps", [P, 8, NC], F32))

        def pair(g):
            k = g.slot(2)
            return ps[:, 2 * k:2 * k + 2, :]

        raw_landed = [sem(f"raw_landed{k}") for k in range(RING)]
        hi_done, lo_done, tile_used = sem("hi_done"), sem("lo_done"), sem("tile_used")
        acc_free = sem("acc_free")
        t_done, t_free = sem("t_done"), sem("t_free")
        ada_landed = [sem(f"ada_landed{k}") for k in range(ADA_RING)]
        ada_used, mod_kept = sem("ada_used"), sem("mod_kept")
        consts_in, x_in, c_in, c_ready = sem("consts_in"), sem("x_in"), sem("c_in"), sem("c_ready")
        norm_sq, norm_var, norm_std, norm_x = sem("norm_sq"), sem("norm_var"), sem("norm_std"), sem("norm_x")
        xt_ready, t_hi = sem("xt_ready"), sem("t_hi")
        a_ready = sem("a_ready")
        proj_in = sem("proj_in")
        dve_chain, act_chain = sem("dve_chain"), sem("act_chain")
        ck_ready, kb_sum, kb_hi_done, kb_ready = sem("ck_ready"), sem("kb_sum"), sem("kb_hi_done"), sem("kb_ready")
        hdn_ready, hdnT_done, hdnT_ready, w2_in = sem("hdn_ready"), sem("hdnT_done"), sem("hdnT_ready"), sem("w2_in")
        cmp_done, kc_roped, kcT_done, cmp_ready = sem("cmp_done"), sem("kc_roped"), sem("kcT_done"), sem("cmp_ready")
        band_in, po_done, po_copied, z_done = sem("band_in"), sem("po_done"), sem("po_copied"), sem("z_done")
        gp_silu, y_pool_ready = sem("gp_silu"), sem("y_pool_ready")
        scale_in, b_in, x1_in, fin_in = sem("scale_in"), sem("b_in"), sem("x1_in"), sem("fin_in")
        gate_sum, gate_ready, gate_used = sem("gate_sum"), sem("gate_ready"), sem("gate_used")
        merged_ready, x1_ready = sem("merged_ready"), sem("x1_ready")
        mod_ready, g_out, g_in = sem("mod_ready"), sem("g_out"), sem("g_in")
        act_ready = sem("act_ready")
        out_ready, out_done = sem("out_ready"), sem("out_done")
        hss_ready, hstd = sem("hss_ready"), sem("hstd")
        bias_in, bias_used = sem("bias_in"), sem("bias_used")

        class Attention:

            def __init__(self, kind, groups, branches, t_groups):
                self.kind, self.groups, self.br, self.tg = kind, groups, branches, t_groups
                self.q_ready = sem(kind + "_q_ready")
                self.sg_ready = sem(kind + "_sg_ready")
                self.v_ready = sem(kind + "_v_ready")
                self.aux_done = sem(kind + "_aux_done")
                self.aux_free = sem(kind + "_aux_free")
                self.qk_done = sem(kind + "_qk_done")
                self.max_ready = sem(kind + "_max_ready")
                self.exp_done = sem(kind + "_exp_done")
                self.p_ready = sem(kind + "_p_ready")
                self.pv_done = sem(kind + "_pv_done")
                self.o_ready = sem(kind + "_o_ready")
                self.y_hi_done = sem(kind + "_y_hi_done")
                self.y_done = sem(kind + "_y_done")

            def keys(self, tb):
                return P * (tb + 1) if self.kind == "nsa" else S

            def rounds(self, tb):
                return [(b, sb) for b in range(self.br) for sb in range(self.keys(tb) // P)]

        nsa = Attention("nsa", NKV, 2, 2 + 2 + 2 + 4)
        gqa = Attention("gqa", 2, 1, 2 + 4)
        na = Attention("na", 2, 1, 2 + 2 + 4)

        TG, n = {}, 0
        for name, k in (("norm1", 8), ("nsa", nsa.tg * nsa.groups), ("pool", 4), ("merged1", 8),
                        ("norm2", 8), ("gqa", gqa.tg * 2), ("na", na.tg * 2), ("merged2", 8),
                        ("norm3", 8), ("ff", 2 * FC)):
            TG[name] = n
            n += k
        TH, n = {}, 0
        for name, k in (("norm1", 8), ("pool", 4), ("merged1", 8), ("norm2", 8), ("merged2", 8), ("norm3", 8),
                        ("ff", 2 * FC)):
            TH[name] = n
            n += k
        XT = {"norm1": 0, "norm2": 8, "norm3": 16}
        CH_NSA = 46

        def score(k, w):
            return ps[:, k // 2, (k % 2) * S:(k % 2) * S + w]

        block = ctx.enter_context(nc.Block())

        @block.sync
        def _(sp):
            ws = t["ws"]
            for k in range(RING):
                sp.dma_start(raw[:, k, :], ws[k]).then_inc(raw_landed[k], 16)
            laps = N_TILES // RING
            with sp.Fori(1, laps) as i:
                for k in range(RING):
                    sp.wait_ge(lo_done, RING * i + (k + 1 - RING))
                    sp.dma_start(raw[:, k, :], ws[RING * i + k]).then_inc(raw_landed[k], 16)
            for tile in range(laps * RING, N_TILES):
                sp.wait_ge(lo_done, tile + 1 - RING)
                sp.dma_start(raw[:, tile % RING, :], ws[tile]).then_inc(raw_landed[tile % RING], 16)
            sp.wait_ge(out_ready, 1)
            for tb in range(TB):
                sp.dma_start(t["out"][tb * P:(tb + 1) * P, :].rearrange("p (c n) -> p c n", c=4),
                             xn[:, :, tb, :]).then_inc(out_done, 16)
            sp.wait_ge(out_done, 32)

        @block.gpsimd
        def _(pool):
            for tb in range(TB):
                pool.dma_start(x0[:, :, tb, :], t["x"][tb * P:(tb + 1) * P, :].rearrange("p (c n) -> p c n", c=4))\
                    .then_inc(x_in, 16)
            small = [(ident, "ident"), (trig1, "trig1"), (trig2, "trig2"), (trigc, "trigc"), (causal, "causal"),
                     (cmask, "cmask"), (cvalid, "cvalid"), (n1T, "n1T"), (n1T_2, "n1T_2"), (n2T_2, "n2T_2"),
                     (peT, "peT"), (b_adaT, "b_adaT")]
            for dst, name in small:
                pool.dma_start(dst[:], t[name]).then_inc(consts_in, 16)
            pool.dma_start(qkn[:], t["qkn"].partition_broadcast(P)).then_inc(consts_in, 16)
            assert len(small) + 1 == N_CONSTS
            pool.dma_start(cb[:], t["c"].partition_broadcast(P)).then_inc(c_in, 16)
            wa = t["wa"]
            for k in range(ADA_RING):
                pool.dma_start(ada[:, k, :], wa[k]).then_inc(ada_landed[k], 16)
            first = (C_IN * ADA_PER_CHUNK["proj"]) // ADA_RING
            with pool.Fori(1, first) as i:
                for k in range(ADA_RING):
                    pool.wait_ge(ada_used, ADA_RING * i + (k + 1 - ADA_RING))
                    pool.dma_start(ada[:, k, :], wa[ADA_RING * i + k]).then_inc(ada_landed[k], 16)
            pool.wait_ge(kb_ready, 2)
            pool.dma_start(w2[:], t["w2"]).then_inc(w2_in, 16)
            pool.wait_ge(nsa.y_done, TB * nsa.groups + 1)
            pool.dma_start(band[:], t["band"]).then_inc(band_in, 16)
            pool.dma_start(mix[:], t["mix"]).then_inc(band_in, 16)
            pool.dma_start(scale_b[:], t["pool_scale"].partition_broadcast(P)).then_inc(scale_in, 16)
            pool.wait_ge(tile_used, T0["merge_a"])
            pool.dma_start(b_b[:], t["b_merge"].partition_broadcast(P)).then_inc(b_in, 16)
            for tb in range(TB):
                pool.dma_start(x1[:, :, tb, :], t["x"][tb * P:(tb + 1) * P, :].rearrange("p (c n) -> p c n", c=4))\
                    .then_inc(x1_in, 16)
            with pool.Fori(first, 2 * N_ADA // ADA_RING) as i:
                for k in range(ADA_RING):
                    pool.wait_ge(ada_used, ADA_RING * i + (k + 1 - ADA_RING))
                    pool.dma_start(ada[:, k, :], wa[ADA_RING * i + k]).then_inc(ada_landed[k], 16)
            pool.wait_ge(tile_used, T0["out1"])
            pool.dma_start(final_b[:], t["final_norm_w"].partition_broadcast(P)).then_inc(fin_in, 16)
            pool.wait_ge(mod_ready, 1)
            for n, part in enumerate((2, 5)):
                pool.dma_start(t["g_rows"][n].rearrange("(k p) -> p k", p=P), mod[:, part * KT:(part + 1) * KT],
                               allow_slow_non_contiguous=True)\
                    .then_inc(g_out, 16)
            for g in range(2):
                for tb in range(TB):
                    u = TB * g + tb
                    if u:
                        pool.wait_ge(bias_used, u)
                    for half in range(2):
                        tr = 2 * tb + half
                        for h in range(4):
                            pool.dma_start(
                                na_bias[64 * half:64 * half + 64, h, :],
                                t["rpb"][4 * g + h, :, (ROWS - 1 - tr) * GRID_W:(2 * ROWS - 1 - tr) * GRID_W])\
                                .then_inc(bias_in, 16)
            pool.wait_ge(g_out, 32)
            pool.wait_ge(na.y_done, TB * na.groups + 1)
            pool.dma_start(g12[:], t["g_rows"].rearrange("a (c n) -> a c n", c=4).partition_broadcast(P)).then_inc(g_in, 16)
            pool.wait_ge(tile_used, T0["out2"])
            pool.dma_start(final_b[:], t["final_w"].partition_broadcast(P)).then_inc(fin_in, 16)

        @block.scalar
        def _(act):
            chain = Count(act_chain)

            def link(ins):
                chain.on(ins)
                act.wait_ge(act_chain, chain.n)

            def split(k):
                act.wait_ge(raw_landed[k.slot(RING)], k.lap(RING, 16))
                if not (k.i is None and k.base < RING):
                    act.wait_ge(tile_used, (k + (1 - RING)).n)
                act.activation(w_hi[:, k.slot(RING), :], raw[:, k.slot(RING), :], ACT.Copy).then_inc(hi_done, 1)

            def steps(k, n, last=N_TILES):
                for j in range(n):
                    if (k + j).i is not None or (k + j).base + RING < last:
                        split(k + (j + RING))

            def t_copy(r, dst, src=None):
                act.wait_ge(t_done, (r + 1).n)
                act.activation(dst, ps[:, 4 + r.slot(2), :] if src is None else src, ACT.Copy).then_inc(t_free, 1)

            def stats(n, x):
                for tb in range(TB):
                    link(act.activation(xn[:, :, tb, :], x[:, :, tb, :], ACT.Square, accum_out=ssq[:, tb:tb + 1]))
                act.sem_inc(norm_sq, 1)
                act.wait_ge(norm_var, n + 1)
                act.activation(rstd[:, :], ssq[:, :], ACT.Sqrt).then_inc(norm_std, 1)

            def modulated_hi(name):
                for r in range(8):
                    act.wait_ge(xt_ready, XT[name] + r + 1)
                    act.activation(a_hi[:, 2 * r:2 * r + 2, :], xt[:, r % 2, :], ACT.Copy).then_inc(t_hi, 1)

            def transposed_hi(r0, n, dst):
                for r in range(n):
                    act.wait_ge(t_done, r0 + r + 1)
                    act.activation(dst(r), ps[:, 4 + (r0 + r) % 2, :], ACT.Copy).then_inc(t_hi, 1)

            def attention(a, i, g, tg):
                u0 = At(g.base * TB, g.per * TB, g.i)
                r = At(tg.base, tg.per, tg.i)
                nsa_, na_ = a.kind == "nsa", a.kind == "na"
                kT = kT1 if nsa_ else kT2
                if nsa_:
                    act.wait_ge(a.pv_done, (u0 + 1).n)
                    act.activation(sg[:], proj[:, 14 + i], ACT.Silu).then_inc(a.sg_ready, 1)
                    for b in range(2):
                        act.activation(vg[:, :, b, :], proj[:, 4 + b, :, bass.ds(i * HD, HD)], ACT.Copy)
                    act.activation(vcg[:], vc[:, i, :], ACT.Copy).then_inc(a.v_ready, 1)
                for h in range(2):
                    t_copy(r, qT[:, 2 * h:2 * h + 2, :])
                    r = r + 1
                if na_:
                    for h in range(2):
                        t_copy(r, kT[:, 2 * h:2 * h + 2, :])
                        r = r + 1
                else:
                    aux = At(g.base * (3 if nsa_ else 1), g.per * 3, g.i)
                    act.wait_ge(a.aux_done, (aux + 1).n)
                    act.activation(kT[:, 0:a.br, :], ps[:, 7, 0:a.br * S], ACT.Copy).then_inc(a.aux_free, 1)
                if nsa_:
                    for h in range(2):
                        t_copy(r, gT[:, 2 * h:2 * h + 2, :])
                        r = r + 1
                rows = 4 * a.br
                for tb in range(TB):
                    u = u0 + tb
                    w = a.keys(tb)
                    act.wait_ge(a.max_ready, (u + 1).n)
                    for k in range(rows):
                        e = act.activation(prob[:, k, 0:w], score(k, w), ACT.Exp, bias=nms[:, k:k + 1],
                                           scale=1.0 if na_ else SCALE, accum_out=den[:, k:k + 1])
                    if nsa_:
                        e = act.activation(pc[:], pc[:], ACT.Exp, scale=SCALE)
                    chain.on(e)
                    act.wait_ge(act_chain, chain.n)
                    act.sem_inc(a.exp_done, 1)
                    for n, _ in enumerate(a.rounds(tb)):
                        t_copy(r, pt[:, n % 2, :])
                        r = r + 1
                    if nsa_:
                        act.wait_ge(a.aux_done, (aux + (2 + tb)).n)
                        act.activation(pcT[:], ps[0:N_CMP, 7, :], ACT.Copy).then_inc(a.aux_free, 1)
                        act.wait_ge(a.o_ready, (u + 1).n)
                        act.activation(y_hi[:, i, :, tb * P:(tb + 1) * P], ot[:].rearrange("p (h s) -> p h s", h=4),
                                       ACT.Copy).then_inc(a.y_hi_done, 1)
                    else:
                        act.wait_ge(a.pv_done, (u + 1 + 1).n)
                        dst = yb_hi if na_ else ya_hi
                        act.activation(dst[:, i, :, tb * P:(tb + 1) * P],
                                       ps[:, 6, :].rearrange("p (h s) -> p h s", h=4),
                                       ACT.Copy).then_inc(a.y_hi_done, 1)

            for a in (nsa, gqa, na):
                act.sem_inc(a.exp_done, 1)
                act.sem_inc(a.y_hi_done, 1)
                act.sem_inc(a.aux_free, 1)
            for k in range(RING):
                split(At(k))
            act.wait_ge(x_in, 32)
            stats(0, x0)
            modulated_hi("norm1")
            act.wait_ge(c_in, 16)
            act.activation(cb[:], cb[:], ACT.Silu).then_inc(c_ready, 1)
            with act.Fori(0, C_IN // 2) as i:
                for c in range(2):
                    k = At(T0["proj"] + c * T_K, 2 * T_K, i)
                    steps(k, T_K)
                    act.activation(proj[:, 2 * i + c], pair(At(G0["proj"] + c, 2, i)), ACT.Copy)\
                        .then_inc(acc_free, 1)
            steps(At(T0["gbr"]), 1)
            act.activation(gates[:], pair(At(G0["gbr"]))[:, :, 0:3 * NQ], ACT.Sigmoid).then_inc(acc_free, 1)
            for r in range(4):
                act.wait_ge(kcT_done, r + 1)
                act.activation(ckT[:, r // 2, 2 * (r % 2):2 * (r % 2) + 2, :], ps[:, 4 + r % 2, :], ACT.Copy)\
                    .then_inc(ck_ready, 1)
            for n, name in enumerate(("cmp_k", "cmp_v")):
                act.wait_ge(kb_sum, n + 1)
                if n:
                    act.wait_ge(tile_used, T0["cmp_v"])
                act.activation(kb_hi[:], kbf[:], ACT.Copy).then_inc(kb_hi_done, 1)
                steps(At(T0[name]), 8)
                act.wait_ge(tile_used, T0[name] + 8)
                act.activation(hdn[:], pair(At(G0[name]))[0:CMP_ROWS, 0, 0:CMP_H], ACT.Silu).then_inc(acc_free, 1)
                act.wait_ge(acc_free, G0[name] + 1 + 2)
                act.sem_inc(hdn_ready, 1)
                act.wait_ge(hdnT_done, n + 1)
                act.activation(hdnT[:, n, :, :], ps[:, 4, 0:2 * CMP_ROWS], ACT.Copy).then_inc(hdnT_ready, 1)
            act.wait_ge(cmp_done, 2)
            act.activation(vc[:], ps[0:N_CMP, 5, :], ACT.Copy).then_inc(cmp_ready, 1)
            act.wait_ge(kcT_done, 5)
            act.activation(kcT[:], ps[:, 7, 0:CMP_ROWS], ACT.Copy).then_inc(cmp_ready, 1)
            act.wait_ge(cmp_ready, 2)

            with turns(act, nsa.groups, chain, 2) as i:
                attention(nsa, i, At(0, 1, i), At(TG["nsa"], nsa.tg, i))

            for c in range(2):
                act.activation(proj[:, 12 + c], proj[:, 12 + c], ACT.Silu).then_inc(gp_silu, 1)
            for r in range(4):
                act.wait_ge(po_done, r + 1)
                act.activation(poT[:, 2 * r:2 * r + 2, :], ps[:, r, :], ACT.Copy).then_inc(po_copied, 1)
            transposed_hi(TG["pool"], 4, lambda r: yp_hi[:, 2 * r:2 * r + 2, :])

            with act.Fori(0, 4) as i:
                steps(At(T0["pool_out"], T_H, i), T_H)
            with act.Fori(0, 2) as i:
                for c in range(2):
                    steps(At(T0["merge_a"] + c * T_K, 2 * T_K, i), T_K)
                    act.wait_ge(gate_sum, 2 * i + c + 1)
                    act.activation(ga[:], ga[:], ACT.Sigmoid).then_inc(gate_ready, 1)
            with act.Fori(0, 4) as i:
                steps(At(T0["merge_b"], 2 * T_K, i), T_K)
                act.wait_ge(gate_sum, i + 5)
                act.activation(ga[:], ga[:], ACT.Sigmoid).then_inc(gate_ready, 1)
                steps(At(T0["merge_b"] + T_K, 2 * T_K, i), T_K)
            transposed_hi(TG["merged1"], 8, lambda r: a_hi[:, 2 * r:2 * r + 2, :])
            with act.Fori(0, 4) as i:
                steps(At(T0["out1"], T_K, i), T_K)

            act.wait_ge(x1_ready, 1)
            stats(1, x1)
            act.wait_ge(x1_ready, 2)
            stats(2, x1)
            modulated_hi("norm2")
            with act.Fori(0, C_IN2) as i:
                steps(At(T0["proj2"], T_K, i), T_K)
            for g in range(2):
                for w in range(2):
                    act.wait_ge(hss_ready, 2 * g + w + 1)
                    act.activation(hss[:, :, 4 * w:4 * w + (1 if w else 4)], hss[:, :, 4 * w:4 * w + (1 if w else 4)],
                                   ACT.Sqrt).then_inc(hstd, 1)
                attention(gqa, g, At(g), At(TG["gqa"] + g * gqa.tg))
            for g in range(2):
                attention(na, g, At(g), At(TG["na"] + g * na.tg))
            with act.Fori(0, 4) as i:
                k = At(T0["merge2"], 2 * T_K + 2 * T_H, i)
                for c in range(2):
                    dst = (ga, gb)[c]
                    steps(k + c * T_K, T_K)
                    g = At(G0["merge2"] + c, 4, i)
                    act.wait_ge(gate_used, i + 1)
                    act.wait_ge(acc_free, (g + 2).n)
                    act.activation(dst[:], pair(g), ACT.Sigmoid).then_inc(acc_free, 1)
                steps(k + 2 * T_K, 2 * T_H)
            transposed_hi(TG["merged2"], 8, lambda r: a_hi[:, 2 * r:2 * r + 2, :])
            with act.Fori(0, 4) as i:
                steps(At(T0["out2"], T_K, i), T_K)
            act.wait_ge(x1_ready, 3)
            stats(3, x1)
            modulated_hi("norm3")

            def gate_up(k, g, j):
                steps(k, T_K)
                act.wait_ge(act_ready, j)
                act.wait_ge(acc_free, (g + 2).n)
                act.activation(f_silu[:], pair(g), ACT.Silu).then_inc(acc_free, 1)
                steps(k + T_K, T_K)

            def act_hi(j):
                for r in range(2):
                    tr = At(TG["ff"] + r, 2, j) if not isinstance(j, int) else At(TG["ff"] + r + 2 * j)
                    act.wait_ge(t_done, (tr + 1).n)
                    act.activation(f_hi[:, 2 * r:2 * r + 2, :], ps[:, 4 + tr.slot(2), :], ACT.Copy).then_inc(t_hi, 1)

            gate_up(At(T0["ff_first"]), At(G0["ff_first"]), 0)
            act_hi(0)
            with act.Fori(1, FC) as j:
                per = 2 * T_K + 4 * T_Q
                gate_up(At(T0["ff"] - per, per, j), At(G0["ff"] - 6, 6, j), j)
                steps(At(T0["ff"] - per + 2 * T_K, per, j), 4 * T_Q)
                act_hi(j)
            steps(At(T0["ff_last"]), 4 * T_Q)
            act.wait_ge(x1_ready, 4)
            stats(4, x1)

        @block.vector
        def _(dve):
            chain = Count(dve_chain)

            def link(ins):
                chain.on(ins)
                dve.wait_ge(dve_chain, chain.n)

            def split(k):
                dve.wait_ge(hi_done, (k + 1).n)
                dve.tensor_tensor(w_lo[:, k.slot(RING), :], raw[:, k.slot(RING), :],
                                  w_hi[:, k.slot(RING), :].bitcast(F32), ALU.subtract).then_inc(lo_done, 1)

            def modulation(k, m):
                dve.wait_ge(ada_landed[k.slot(ADA_RING)], k.lap(ADA_RING, 16))
                a = ada[:, k.slot(ADA_RING), :]
                half = k.base % 2
                assert k.per % 2 == 0
                dve.tensor_tensor_reduce(out=a, in0=a, in1=cb[:, half * TW:(half + 1) * TW], scale=1.0, scalar=0.0,
                                         op0=ALU.mult, op1=ALU.add, accum_out=mod_part[:, m:m + 1])\
                    .then_inc(ada_used, 1)

            def keep_modulation(a, n, kept):
                dve.wait_ge(ada_used, (a + n).n)
                dve.tensor_copy(mod2[:, bass.ds(a.n, n)], mod_part[:, 0:n]).then_inc(mod_kept, 1)
                dve.wait_ge(mod_kept, (kept + 1).n)

            def steps(k, n, a=None, na_=0, kept=None, last=N_TILES):
                done = 0
                for j in range(n):
                    if (k + j).i is not None or (k + j).base + RING < last:
                        split(k + (j + RING))
                    while done * n < na_ * (j + 1) and done < na_:
                        modulation(a + done, done)
                        done += 1
                if na_:
                    keep_modulation(a, na_, kept)

            def stats(n):
                dve.wait_ge(norm_sq, n + 1)
                dve.tensor_scalar(ssq[:, :], ssq[:, :], 1.0 / D, EPS, ALU.mult, ALU.add).then_inc(norm_var, 1)
                dve.wait_ge(norm_std, n + 1)
                link(dve.reciprocal(rstd[:, :], rstd[:, :]))

            def norm(n, x):
                stats(n)
                for tb in range(TB):
                    dve.tensor_scalar(xn[:, :, tb, :], x[:, :, tb, :], rstd[:, tb:tb + 1], None, ALU.mult)\
                        .then_inc(norm_x, 1)

            def modulated_lo(name, scale, shift):
                for r in range(8):
                    tg, th = TG[name] + r, TH[name] + r
                    dve.wait_ge(t_done, tg + 1)
                    if r >= 2:
                        dve.wait_ge(t_hi, th - 1)
                    for k in range(2):
                        chain.on(dve.tensor_scalar(
                            xt[:, r % 2, k * S:(k + 1) * S], ps[:, 4 + tg % 2, k * S:(k + 1) * S],
                            scale[:, 2 * r + k:2 * r + k + 1], shift(2 * r + k), ALU.mult, ALU.add))
                    dve.wait_ge(dve_chain, chain.n)
                    dve.sem_inc(xt_ready, 1)
                    dve.wait_ge(t_hi, th + 1)
                    dve.tensor_tensor(a_lo[:, 2 * r:2 * r + 2, :], xt[:, r % 2, :],
                                      a_hi[:, 2 * r:2 * r + 2, :].bitcast(F32), ALU.subtract).then_inc(t_free, 1)

            def transposed_lo(r0, h0, n, hi, lo):
                for r in range(n):
                    dve.wait_ge(t_hi, h0 + r + 1)
                    dve.tensor_tensor(lo(r), ps[:, 4 + (r0 + r) % 2, :], hi(r).bitcast(F32), ALU.subtract)\
                        .then_inc(t_free, 1)

            def rope(src, dst, tmp, trig, bcast):
                cos, sin = bcast(trig, 0), bcast(trig, 1)
                for n, (s, tr) in enumerate(((src[0], cos), (src[1], sin), (src[1], cos), (src[0], sin))):
                    chain.on(dve.tensor_tensor(tmp[n], s, tr, ALU.mult))
                dve.wait_ge(dve_chain, chain.n)
                chain.on(dve.tensor_tensor(dst[0], tmp[0], tmp[1], ALU.subtract))
                chain.on(dve.tensor_tensor(dst[1], tmp[2], tmp[3], ALU.add))
                dve.wait_ge(dve_chain, chain.n)

            def heads(x, h):
                return x[:, :, 0:h, 0:HALF], x[:, :, 0:h, HALF:HD]

            def attention(a, i, g):
                u0 = At(g.base * TB, g.per * TB, g.i)
                nsa_, na_ = a.kind == "nsa", a.kind == "na"
                if not na_:
                    dve.wait_ge(a.pv_done, (u0 + 1).n)
                    dve.wait_ge(a.y_hi_done, (u0 + 1).n)
                    trig = trig1 if nsa_ else trig2

                    def b4(tr, which):
                        return tr[:, which].unsqueeze(2).to_broadcast([P, TB, 4, HALF])

                    def b1(tr, which):
                        return tr[:, which]

                    tq = [rt[:, n] for n in range(4)]
                    tk = [rt[:, n, :, 0, :] for n in range(4)]
                    if nsa_:
                        q = proj[:, 6 + i].rearrange("p t (h d) -> p t h d", h=4)
                        rope(heads(q, 4), heads(qr, 4), tq, trig, b4)
                        for b in range(2):
                            k = proj[:, 2 + b, :, bass.ds(i * HD, HD)]
                            rope((k[:, :, 0:HALF], k[:, :, HALF:HD]),
                                 (kr1[:, :, b, 0:HALF], kr1[:, :, b, HALF:HD]), tk, trig, b1)
                    else:
                        q = proj[:, i].rearrange("p t (h d) -> p t h d", h=4)
                        k = proj[:, 2, :, i * HD:(i + 1) * HD]
                        for w, (x, dst, n) in enumerate(((q, qr[:], 4), (k.unsqueeze(2), kr2[:].unsqueeze(2), 1))):
                            s = hss[:, :, 4 * w:4 * w + n]
                            link(dve.tensor_tensor(dst, x, x, ALU.mult))
                            link(dve.tensor_reduce(s, dst, AX.X, ALU.add))
                            dve.tensor_scalar(s, s, 1.0 / HD, EPS, ALU.mult, ALU.add).then_inc(hss_ready, 1)
                            dve.wait_ge(hstd, 2 * i + w + 1)
                            link(dve.reciprocal(s, s))
                            link(dve.tensor_tensor(dst, x, s.unsqueeze(3).to_broadcast([P, TB, n, HD]), ALU.mult))
                            link(dve.tensor_tensor(dst, dst, qkn[:, w].unsqueeze(1).unsqueeze(1)
                                                   .to_broadcast([P, TB, n, HD]), ALU.mult))
                        rope(heads(qr, 4), heads(qr, 4), tq, trig, b4)
                        rope((kr2[:, :, 0:HALF], kr2[:, :, HALF:HD]), (kr2[:, :, 0:HALF], kr2[:, :, HALF:HD]),
                             tk, trig, b1)
                    dve.sem_inc(a.q_ready, 1)
                rows = 4 * a.br
                for tb in range(TB):
                    u = u0 + tb
                    w = a.keys(tb)
                    sc = ps[:, 0:rows // 2, :].rearrange("p b (k s) -> p (b k) s", s=S)
                    dve.wait_ge(a.qk_done, (u + 1).n)
                    if nsa_:
                        diag = sc[:, :, w - P:w]
                        chain.on(dve.tensor_tensor(diag, diag, causal[:].unsqueeze(1).to_broadcast([P, rows, P]), ALU.add))
                        small = ps[:, 6, 0:4 * N_CMP].rearrange("p (h n) -> p h n", h=4)
                        chain.on(dve.tensor_tensor(pc[:], small, cmask[:, tb].unsqueeze(1).to_broadcast([P, 4, N_CMP]),
                                                   ALU.add))
                        dve.wait_ge(dve_chain, chain.n)
                        chain.on(dve.tensor_reduce(cmx[:], pc[:], AX.X, ALU.max))
                    if na_:
                        dve.wait_ge(bias_in, (u + 1).n * 16 * 8)
                        link(dve.scalar_tensor_tensor(out=sc, in0=sc, scalar=SCALE, in1=na_bias[:],
                                                      op0=ALU.mult, op1=ALU.add))
                    chain.on(dve.tensor_reduce(nmax[:, 0:rows], sc[:, :, 0:w], AX.X, ALU.max))
                    dve.wait_ge(dve_chain, chain.n)
                    if na_:
                        dve.sem_inc(bias_used, 1)
                    if nsa_:
                        chain.on(dve.tensor_tensor(pc[:], pc[:], cmx[:].unsqueeze(2).to_broadcast([P, 4, N_CMP]),
                                                   ALU.subtract))
                    chain.on(dve.tensor_scalar(nms[:, 0:rows], nmax[:, 0:rows], -1.0 if na_ else -SCALE, None, ALU.mult))
                    dve.wait_ge(dve_chain, chain.n)
                    dve.sem_inc(a.max_ready, 1)
                    dve.wait_ge(a.exp_done, (u + 1 + 1).n)
                    link(dve.reciprocal(den[:, 0:rows], den[:, 0:rows]))
                    if nsa_:
                        chain.on(dve.tensor_reduce(cden[:], pc[:], AX.X, ALU.add))
                        dve.wait_ge(dve_chain, chain.n)
                        gate = gates[:, tb, bass.ds(12 * i, 12)].rearrange("p (h b) -> p h b", b=3)
                        chain.on(dve.tensor_tensor(coef[:].rearrange("p (h b) -> p h b", b=2),
                                                   den[:].rearrange("p (h b) -> p h b", b=2), gate[:, :, 1:3], ALU.mult))
                        chain.on(dve.reciprocal(cden[:], cden[:]))
                        dve.wait_ge(dve_chain, chain.n)
                        link(dve.tensor_tensor(cden[:], cden[:], gate[:, :, 0], ALU.mult))
                        chain.on(dve.tensor_tensor(pc[:], pc[:], cvalid[:, tb].unsqueeze(1).to_broadcast([P, 4, N_CMP]),
                                                   ALU.mult))
                        dve.wait_ge(dve_chain, chain.n)
                        chain.on(dve.tensor_tensor(pc[:], pc[:], cden[:].unsqueeze(2).to_broadcast([P, 4, N_CMP]),
                                                   ALU.mult))
                    cf = coef if nsa_ else den
                    chain.on(dve.tensor_tensor(prob[:, 0:rows, 0:w], prob[:, 0:rows, 0:w],
                                               cf[:, 0:rows].unsqueeze(2).to_broadcast([P, rows, w]), ALU.mult))
                    dve.wait_ge(dve_chain, chain.n)
                    dve.sem_inc(a.p_ready, 1)
                    o = ps[:, 6, :].rearrange("p (h s) -> p h s", h=4)
                    dst = {"nsa": (y_hi, y_lo), "gqa": (ya_hi, ya_lo), "na": (yb_hi, yb_lo)}[a.kind]
                    hi, lo = (d[:, i, :, tb * P:(tb + 1) * P] for d in dst)
                    if nsa_:
                        dve.wait_ge(a.pv_done, (u + 1 + 1).n)
                        o = ot[:].rearrange("p (h s) -> p h s", h=4)
                        dve.tensor_tensor(o, ps[:, 6, :].rearrange("p (h s) -> p h s", h=4),
                                          gT[:, :, tb * P:(tb + 1) * P], ALU.mult).then_inc(a.o_ready, 1)
                    dve.wait_ge(a.y_hi_done, (u + 1 + 1).n)
                    dve.tensor_tensor(lo, o, hi.bitcast(F32), ALU.subtract).then_inc(a.y_done, 1)

            for a in (nsa, gqa, na):
                dve.sem_inc(a.y_done, 1)
            dve.sem_inc(gate_used, 1)
            dve.memset(nmax[:, :], 0.0).then_inc(acc_free, 2)
            dve.memset(cmx[:, :], 0.0).then_inc(t_free, 2)
            for k in range(RING):
                split(At(k))
            dve.wait_ge(consts_in, 16 * N_CONSTS)
            norm(0, x0)
            modulated_lo("norm1", n1T, lambda k: 0.0)
            dve.wait_ge(c_ready, 1)
            with dve.Fori(0, C_IN // 2) as i:
                n = ADA_PER_CHUNK["proj"]
                steps(At(T0["proj"], 2 * T_K, i), 2 * T_K, At(ADA0["proj"], 2 * n, i), 2 * n, At(0, 1, i))
            steps(At(T0["gbr"]), 1)
            dve.wait_ge(ck_ready, 4)
            for n, name in enumerate(("cmp_k", "cmp_v")):
                if n:
                    dve.wait_ge(kb_hi_done, 1)
                for half in range(2):
                    src = ckT[:, n].rearrange("p h (m l) -> p h m l", l=CMP_STRIDE)[:, :, half:half + N_CMP, :]
                    ls = slice(half * CMP_STRIDE, (half + 1) * CMP_STRIDE)
                    dst = kbf[:, ls, :].rearrange("p l (h m) -> p h m l", h=NKV)
                    for h in range(NKV):
                        ins = dve.tensor_tensor(dst[:, h], src[:, h],
                                                peT[:, n, ls].unsqueeze(1).to_broadcast([P, N_CMP, CMP_STRIDE]), ALU.add)
                        chain.on(ins)
                dve.wait_ge(dve_chain, chain.n)
                dve.sem_inc(kb_sum, 1)
                dve.wait_ge(kb_hi_done, n + 1)
                dve.tensor_tensor(kb_lo[:], kbf[:], kb_hi[:].bitcast(F32), ALU.subtract).then_inc(kb_ready, 1)
                steps(At(T0[name]), 8)
            dve.wait_ge(cmp_done, 1)
            link(dve.tensor_copy(kcr[:], ps[0:N_CMP, 6, :].rearrange("p (h d) -> p h d", h=NKV)))
            rope((kcr[:, :, 0:HALF], kcr[:, :, HALF:HD]), (kcr[:, :, 0:HALF], kcr[:, :, HALF:HD]),
                 [kct[:, n] for n in range(4)], trigc,
                 lambda tr, which: tr[:, which].unsqueeze(1).to_broadcast([N_CMP, NKV, HALF]))
            dve.sem_inc(kc_roped, 1)

            with turns(dve, nsa.groups, chain, CH_NSA) as i:
                attention(nsa, i, At(0, 1, i))

            dve.wait_ge(gp_silu, 2)
            dve.wait_ge(scale_in, 16)
            for c in range(2):
                g = proj[:, 12 + c]
                chain.on(dve.tensor_tensor(g, g, scale_b[:, c].unsqueeze(1).to_broadcast([P, TB, NC]), ALU.mult))
            for c in range(2):
                dve.wait_ge(z_done, c + 1)
                dve.wait_ge(dve_chain, chain.n)
                g = proj[:, 12 + c]
                dve.tensor_tensor(g, ps[:, 2 * c:2 * c + 2, :], g, ALU.mult).then_inc(y_pool_ready, 1)
            transposed_lo(TG["pool"], TH["pool"], 4, lambda r: yp_hi[:, 2 * r:2 * r + 2, :],
                          lambda r: yp_lo[:, 2 * r:2 * r + 2, :])

            with dve.Fori(0, 2) as i:
                for c in range(2):
                    k = At(T0["pool_out"] + c * T_H, 2 * T_H, i)
                    steps(k, T_H)
                    dve.wait_ge(tile_used, (k + T_H).n)
                    dve.tensor_copy(ya[:, 2 * i + c], pair(At(G0["pool_out"] + c, 2, i))).then_inc(acc_free, 1)
            dve.wait_ge(b_in, 16)

            def gate(col, g, k, first):
                dve.wait_ge(tile_used, k.n)
                dve.tensor_tensor(ga[:], pair(g), b_b[:, col].unsqueeze(1).to_broadcast([P, TB, NC]), ALU.add)\
                    .then_inc(acc_free, 1)

            with turns(dve, 2, chain, 2) as i:
                n = ADA_PER_CHUNK["merge_a"]
                for c in range(2):
                    k = At(T0["merge_a"] + c * T_K, 2 * T_K, i)
                    steps(k, T_K, At(ADA0["merge_a"] + c * n, 2 * n, i), n, At(9 + c, 2, i))
                    gate(2 * i + c, At(G0["merge_a"] + c, 2, i), k + T_K, c)
                    dve.wait_ge(acc_free, (At(G0["merge_a"] + c, 2, i) + 3).n)
                    dve.sem_inc(gate_sum, 1)
                    dve.wait_ge(gate_ready, 2 * i + c + 1)
                    link(dve.tensor_tensor(ya[:, 2 * i + c], ya[:, 2 * i + c], ga[:], ALU.mult))
            with turns(dve, 4, chain, 1) as i:
                n = ADA_PER_CHUNK["merge_b"]
                k = At(T0["merge_b"], 2 * T_K, i)
                g = At(G0["merge_b"], 2, i)
                steps(k, T_K, At(ADA0["merge_b"], 2 * n, i), n, At(13, 2, i))
                gate(i + 4, g, k + T_K, 0)
                dve.wait_ge(acc_free, (g + 3).n)
                dve.sem_inc(gate_sum, 1)
                steps(k + T_K, T_K, At(ADA0["merge_b"] + n, 2 * n, i), n, At(14, 2, i))
                dve.wait_ge(gate_ready, i + 5)
                dve.wait_ge(tile_used, (k + 2 * T_K).n)
                ins = dve.tensor_tensor(ga[:], pair(g + 1), ga[:], ALU.mult)
                ins.then_inc(acc_free, 1)
                dve.wait_ge(acc_free, (g + 4).n)
                link(dve.tensor_tensor(ya[:, i], ya[:, i], ga[:], ALU.add))
            dve.sem_inc(merged_ready, 1)
            transposed_lo(TG["merged1"], TH["merged1"], 8, lambda r: a_hi[:, 2 * r:2 * r + 2, :],
                          lambda r: a_lo[:, 2 * r:2 * r + 2, :])
            dve.wait_ge(x1_in, 32)
            with dve.Fori(0, 2) as i:
                n = ADA_PER_CHUNK["out1"]
                for c in range(2):
                    k = At(T0["out1"] + c * T_K, 2 * T_K, i)
                    steps(k, T_K)
                    a = At(ADA0["out1"] + c * n, 2 * n, i)
                    for m in range(n):
                        modulation(a + m, m)
                    keep_modulation(a, n, At(21 + c, 2, i))
                    dve.wait_ge(tile_used, (k + T_K).n)
                    x = x1[:, 2 * i + c]
                    dve.tensor_tensor(x, pair(At(G0["out1"] + c, 2, i)), x, ALU.add).then_inc(acc_free, 1)
            dve.wait_ge(acc_free, G0["out1"] + 4 + 2)
            dve.sem_inc(x1_ready, 1)
            stats(1)
            dve.wait_ge(fin_in, 16)
            for tb in range(TB):
                chain.on(dve.scalar_tensor_tensor(out=x1[:, :, tb, :], in0=x1[:, :, tb, :], scalar=rstd[:, tb:tb + 1],
                                                  in1=final_b[:], op0=ALU.mult, op1=ALU.mult))
            dve.wait_ge(dve_chain, chain.n)
            dve.sem_inc(x1_ready, 1)
            dve.wait_ge(mod_kept, C_IN // 2 + 4 + 8 + 4)
            link(dve.tensor_tensor(mod[:], mod2[:].rearrange("p (n h) -> p n h", h=2)[:, :, 0],
                                   mod2[:].rearrange("p (n h) -> p n h", h=2)[:, :, 1], ALU.add))
            link(dve.tensor_tensor(mod[:], mod[:], b_adaT[:], ALU.add))
            dve.sem_inc(mod_ready, 1)
            chain.on(dve.scalar_tensor_tensor(out=scale1[:], in0=mod[:, KT:2 * KT], scalar=1.0, in1=n1T_2[:],
                                              op0=ALU.add, op1=ALU.mult))
            chain.on(dve.scalar_tensor_tensor(out=scale2[:], in0=mod[:, 4 * KT:5 * KT], scalar=1.0, in1=n2T_2[:],
                                              op0=ALU.add, op1=ALU.mult))
            dve.wait_ge(dve_chain, chain.n)
            norm(2, x1)
            modulated_lo("norm2", scale1, lambda k: mod[:, k:k + 1])

            def copy_out(c, k, g):
                dve.wait_ge(tile_used, (k + T_K).n)
                dve.tensor_copy(proj[:, c], pair(g)).then_inc(acc_free, 1)

            with dve.Fori(0, C_IN2 // 2) as i:
                for c in range(2):
                    k = At(T0["proj2"] + c * T_K, 2 * T_K, i)
                    steps(k, T_K)
                    copy_out(2 * i + c, k, At(G0["proj2"] + c, 2, i))
            k = At(T0["proj2"] + (C_IN2 - 1) * T_K)
            steps(k, T_K)
            copy_out(C_IN2 - 1, k, At(G0["proj2"] + C_IN2 - 1))
            dve.wait_ge(acc_free, G0["merge2"] + 2)
            dve.sem_inc(proj_in, 1)
            for a in (gqa, na):
                for g in range(2):
                    attention(a, g, At(g))

            with turns(dve, 4, chain, 1) as i:
                per = 2 * T_K + 2 * T_H
                k = At(T0["merge2"], per, i)
                g = At(G0["merge2"], 4, i)
                steps(k, 2 * T_K + T_H)
                dve.wait_ge(acc_free, (g + 4).n)
                dve.wait_ge(tile_used, (k + (2 * T_K + T_H)).n)
                ins = dve.tensor_tensor(ga[:], pair(g + 2), ga[:], ALU.mult)
                ins.then_inc(acc_free, 1)
                steps(k + (2 * T_K + T_H), T_H)
                dve.wait_ge(tile_used, (k + per).n)
                ins = dve.tensor_tensor(gb[:], pair(g + 3), gb[:], ALU.mult)
                ins.then_inc(acc_free, 1)
                dve.wait_ge(acc_free, (g + 6).n)
                link(dve.tensor_tensor(ya[:, i], ga[:], gb[:], ALU.add))
                dve.sem_inc(gate_used, 1)
            dve.wait_ge(dve_chain, chain.n)
            dve.sem_inc(merged_ready, 1)
            transposed_lo(TG["merged2"], TH["merged2"], 8, lambda r: a_hi[:, 2 * r:2 * r + 2, :],
                          lambda r: a_lo[:, 2 * r:2 * r + 2, :])
            dve.wait_ge(g_in, 16)
            with turns(dve, 2, chain, 2) as i:
                for c in range(2):
                    k = At(T0["out2"] + c * T_K, 2 * T_K, i)
                    g = At(G0["out2"] + c, 2, i)
                    steps(k, T_K)
                    dve.wait_ge(tile_used, (k + T_K).n)
                    ins = dve.tensor_tensor(gb[:], pair(g), g12[:, 0, 2 * i + c, :].unsqueeze(1).to_broadcast([P, TB, NC]),
                                            ALU.mult)
                    ins.then_inc(acc_free, 1)
                    dve.wait_ge(acc_free, (g + 3).n)
                    x = x1[:, 2 * i + c]
                    link(dve.tensor_tensor(x, x, gb[:], ALU.add))
            dve.sem_inc(x1_ready, 1)
            norm(3, x1)
            modulated_lo("norm3", scale2, lambda k: mod[:, 3 * KT + k:3 * KT + k + 1])
            link(dve.memset(acc[:], 0.0))

            def gate_up(k, g, j):
                steps(k, 2 * T_K)
                dve.wait_ge(acc_free, (g + 3).n)
                dve.wait_ge(tile_used, (k + 2 * T_K).n)
                dve.tensor_tensor(f_act[:], pair(g + 1), f_silu[:], ALU.mult).then_inc(acc_free, 1)
                dve.wait_ge(acc_free, (g + 4).n)
                dve.sem_inc(act_ready, 1)

            def down(k, g, last=False):
                for c in range(4):
                    steps(k + c * T_Q, T_Q)
                    dve.wait_ge(tile_used, (k + (c + 1) * T_Q).n)
                    dve.tensor_tensor(acc[:, c], pair(g + c), acc[:, c], ALU.add).then_inc(acc_free, 1)

            def act_lo(j):
                for r in range(2):
                    tr = At(TG["ff"] + r, 2, j) if not isinstance(j, int) else At(TG["ff"] + r + 2 * j)
                    h = At(TH["ff"] + r, 2, j) if not isinstance(j, int) else At(TH["ff"] + r + 2 * j)
                    dve.wait_ge(t_hi, (h + 1).n)
                    dve.tensor_tensor(f_lo[:, 2 * r:2 * r + 2, :], ps[:, 4 + tr.slot(2), :],
                                      f_hi[:, 2 * r:2 * r + 2, :].bitcast(F32), ALU.subtract).then_inc(t_free, 1)

            gate_up(At(T0["ff_first"]), At(G0["ff_first"]), 0)
            act_lo(0)
            with dve.Fori(1, FC) as j:
                per = 2 * T_K + 4 * T_Q
                gate_up(At(T0["ff"] - per, per, j), At(G0["ff"] - 6, 6, j), j)
                down(At(T0["ff"] - per + 2 * T_K, per, j), At(G0["ff"] - 6 + 2, 6, j))
                act_lo(j)
            down(At(T0["ff_last"]), At(G0["ff_last"]))
            dve.wait_ge(acc_free, G0["ff_last"] + 4 + 2)
            for c in range(4):
                chain.on(dve.tensor_tensor(acc[:, c], acc[:, c], g12[:, 1, c, :].unsqueeze(1).to_broadcast([P, TB, NC]),
                                           ALU.mult))
            dve.wait_ge(dve_chain, chain.n)
            link(dve.tensor_tensor(x1[:], x1[:], acc[:], ALU.add))
            dve.sem_inc(x1_ready, 1)
            norm(4, x1)
            dve.wait_ge(norm_x, 8)
            dve.wait_ge(fin_in, 32)
            for c in range(4):
                chain.on(dve.tensor_tensor(xn[:, c], xn[:, c], final_b[:, c].unsqueeze(1).to_broadcast([P, TB, NC]), ALU.mult))
            dve.wait_ge(dve_chain, chain.n)
            dve.sem_inc(out_ready, 1)

        @block.tensor
        def _(pe):
            def gemm(k, g, hi, lo, tiles, kts=2, rows=P, blocks=TB, width=NC):
                pe.wait_ge(acc_free, (g + 1).n)
                n = 0
                out = pair(g)
                for j in range(tiles):
                    pe.wait_ge(lo_done, (k + (j + 1)).n)
                    s = (k + j).slot(RING)
                    for q in range(kts):
                        cols = slice(q * width, (q + 1) * width)
                        for tb in range(blocks):
                            first, last = n == 0, n == tiles * kts - 1
                            o = out[0:rows, tb, 0:width]
                            pe.matmul(o, hi(n, tb), w_hi[:, s, cols], start=first, stop=False)
                            pe.matmul(o, hi(n, tb), w_lo[:, s, cols], start=False, stop=False)
                            mm = pe.matmul(o, lo(n, tb), w_hi[:, s, cols], start=False, stop=last)
                        n += 1
                    mm.then_inc(tile_used, 1)

            def part(x):
                return lambda n, tb: x[:, n, tb * P:(tb + 1) * P]

            def part4(x):
                return lambda n, tb: x[:, n // 4, n % 4, tb * P:(tb + 1) * P]

            def turn(r, blocks, bank=None):
                if bank is None:
                    pe.wait_ge(t_free, (r + 1).n)
                    bank = 4 + r.slot(2)
                for n, b in enumerate(blocks):
                    m = b.shape[-1]
                    ins = pe.transpose(ps[0:m, bank, n * P:n * P + b.shape[0]], b, ident[0:b.shape[0], 0:b.shape[0]])
                return ins

            def turn_chunked(r0, x, n, ready=None):
                for r in range(n):
                    blocks = [x[:, (2 * r + k) // 4, tb, ((2 * r + k) % 4) * P:((2 * r + k) % 4 + 1) * P]
                              for k in range(2) for tb in range(TB)]
                    turn(At(r0 + r), blocks).then_inc(t_done, 1)

            def attention(a, i, g, tg):
                u0 = At(g.base * TB, g.per * TB, g.i)
                r = At(tg.base, tg.per, tg.i)
                nsa_, na_ = a.kind == "nsa", a.kind == "na"
                kT = kT1 if nsa_ else kT2
                if na_:
                    q = proj[:, 3 + i].rearrange("p t (h d) -> p t h d", h=4)
                else:
                    q = qr
                    pe.wait_ge(a.q_ready, (g + 1).n)
                for h in range(2):
                    turn(r, [q[:, tb, 2 * h + k, :] for k in range(2) for tb in range(TB)]).then_inc(t_done, 1)
                    r = r + 1
                if na_:
                    k_ = proj[:, 5 + i].rearrange("p t (h d) -> p t h d", h=4)
                    for h in range(2):
                        turn(r, [k_[:, tb, 2 * h + k, :] for k in range(2) for tb in range(TB)]).then_inc(t_done, 1)
                        r = r + 1
                else:
                    aux = At(g.base * (3 if nsa_ else 1), g.per * 3, g.i)
                    pe.wait_ge(a.aux_free, (aux + 1).n)
                    ks = [kr1[:, tb, b, :] for b in range(2) for tb in range(TB)] if nsa_ else \
                        [kr2[:, tb, :] for tb in range(TB)]
                    turn(r, ks, bank=7).then_inc(a.aux_done, 1)
                if nsa_:
                    pe.wait_ge(a.sg_ready, (g + 1).n)
                    for h in range(2):
                        turn(r, [sg[:, tb, (2 * h + k) * HD:(2 * h + k + 1) * HD] for k in range(2) for tb in range(TB)])\
                            .then_inc(t_done, 1)
                        r = r + 1
                    pe.wait_ge(a.v_ready, (g + 1).n)
                pe.wait_ge(t_free, (r + 2).n)
                if not na_:
                    pe.wait_ge(a.aux_free, (aux + 1 + 1).n)
                for tb in range(TB):
                    u = u0 + tb
                    w = a.keys(tb)
                    pe.wait_ge(a.exp_done, (u + 1).n)
                    pe.wait_ge(a.y_done, (u + 1).n)
                    for h in range(4):
                        lhs = qT[:, h, tb * P:(tb + 1) * P]
                        if nsa_:
                            out = ps[:, h, :].rearrange("p (b s) -> p b s", b=2)[:, :, 0:w]
                            mm = pe.matmul(out, lhs, kT[:, 0:2, 0:w], start=True, stop=True)
                            mm = pe.matmul(ps[:, 6, h * N_CMP:(h + 1) * N_CMP], lhs,
                                           kcT[:, bass.ds(i * N_CMP, N_CMP)], start=True, stop=True)
                        else:
                            mm = pe.matmul(ps[:, h // 2, (h % 2) * S:(h % 2 + 1) * S], lhs,
                                           kT[:, h if na_ else 0, :], start=True, stop=True)
                    mm.then_inc(a.qk_done, 1)
                    pe.wait_ge(a.p_ready, (u + 1).n)
                    rounds = a.rounds(tb)
                    if nsa_:
                        pe.wait_ge(a.aux_free, (aux + (1 + tb) + 1).n)

                    def transposes(n, r=r):
                        b, sb = rounds[n]
                        turn(r + n, [prob[:, h * a.br + b, sb * P:(sb + 1) * P] for h in range(4)]).then_inc(t_done, 1)

                    transposes(0)
                    if nsa_:
                        turn(r, [pc[:, h, :] for h in range(4)], bank=7).then_inc(a.aux_done, 1)
                    for n, (b, sb) in enumerate(rounds):
                        if n + 1 < len(rounds):
                            transposes(n + 1)
                        pe.wait_ge(t_free, (r + (n + 3)).n)
                        first, last = n == 0, n == len(rounds) - 1 and not nsa_
                        if na_:
                            for h in range(4):
                                v = proj[:, 7 + i, sb, h * HD:(h + 1) * HD]
                                mm = pe.matmul(ps[:, 6, h * P:(h + 1) * P], v, pt[:, n % 2, h * P:(h + 1) * P],
                                               start=first and h == 0, stop=last, skip_group_check=True)
                        else:
                            v = vg[:, sb, b, :] if nsa_ else proj[:, 2, sb, 256 + i * HD:256 + (i + 1) * HD]
                            mm = pe.matmul(ps[:, 6, :], v, pt[:, n % 2, :], start=first, stop=last)
                    if nsa_:
                        pe.wait_ge(a.aux_free, (aux + (2 + tb) + 1).n)
                        mm = pe.matmul(ps[:, 6, :], vcg[:], pcT[:], start=False, stop=True)
                    mm.then_inc(a.pv_done, 1)
                    r = r + len(rounds)

            for a in (nsa, gqa, na):
                pe.sem_inc(a.pv_done, 1)
            pe.wait_ge(consts_in, 16 * N_CONSTS)
            pe.wait_ge(norm_x, 2)
            turn_chunked(TG["norm1"], xn, 8)
            pe.wait_ge(t_free, TG["nsa"] + 2)
            ah, al = part(a_hi), part(a_lo)
            with pe.Fori(0, C_IN // 2) as i:
                for c in range(2):
                    gemm(At(T0["proj"] + c * T_K, 2 * T_K, i), At(G0["proj"] + c, 2, i), ah, al, T_K)
            gemm(At(T0["gbr"]), At(G0["gbr"]), ah, al, 1, kts=KT, width=3 * NQ)
            pe.wait_ge(acc_free, C_IN + 2)
            for r in range(4):
                if r >= 2:
                    pe.wait_ge(ck_ready, r - 1)
                blocks = [proj[:, r // 2, tb, (2 * (r % 2) + k) * HD:(2 * (r % 2) + k + 1) * HD]
                          for k in range(2) for tb in range(TB)]
                turn(None, blocks, bank=4 + r % 2).then_inc(kcT_done, 1)
            for n, name in enumerate(("cmp_k", "cmp_v")):
                pe.wait_ge(kb_ready, n + 1)
                gemm(At(T0[name]), At(G0[name]), lambda m, tb: kb_hi[:, m, :], lambda m, tb: kb_lo[:, m, :], 8,
                     kts=4, rows=CMP_ROWS, blocks=1, width=CMP_H)
                pe.wait_ge(hdn_ready, n + 1)
                for f in range(2):
                    ins = pe.transpose(ps[:, 4, f * CMP_ROWS:(f + 1) * CMP_ROWS], hdn[:, f * P:(f + 1) * P],
                                       ident[0:CMP_ROWS, 0:CMP_ROWS])
                ins.then_inc(hdnT_done, 1)
                pe.wait_ge(hdnT_ready, n + 1)
            pe.wait_ge(w2_in, 16)
            for n in range(2):
                for h in range(NKV):
                    for f in range(2):
                        mm = pe.matmul(ps[0:N_CMP, 6 - n, h * HD:(h + 1) * HD],
                                       hdnT[:, n, f, h * N_CMP:(h + 1) * N_CMP], w2[:, n, f, :],
                                       start=f == 0, stop=f == 1)
                mm.then_inc(cmp_done, 1)
            pe.wait_ge(kc_roped, 1)
            for h in range(NKV):
                ins = pe.transpose(ps[:, 7, h * N_CMP:(h + 1) * N_CMP], kcr[:, h, :], ident[0:N_CMP, 0:N_CMP])
            ins.then_inc(kcT_done, 1)
            pe.wait_ge(cmp_ready, 2)

            with pe.Fori(0, nsa.groups) as i:
                attention(nsa, i, At(0, 1, i), At(TG["nsa"], nsa.tg, i))

            pe.wait_ge(nsa.y_done, TB * nsa.groups + 1)

            pe.wait_ge(band_in, 32)
            for ct in range(8):
                for tb in range(TB):
                    mm = pe.matmul(ps[:, ct // 2, (ct % 2) * S:(ct % 2 + 1) * S],
                                   proj[:, 10 + ct // 4, tb, (ct % 4) * P:(ct % 4 + 1) * P],
                                   band[:, ct // 2, tb, :], start=tb == 0, stop=tb == 1)
                if ct % 2:
                    mm.then_inc(po_done, 1)
            pe.wait_ge(po_copied, 4)
            for g in range(4):
                for tb in range(TB):
                    for kk in range(2):
                        mm = pe.matmul(ps[:, 2 * (g // 2) + tb, (g % 2) * POOL_G:(g % 2 + 1) * POOL_G],
                                       poT[:, 2 * g + kk, tb * P:(tb + 1) * P], mix[:, g, kk, :],
                                       start=kk == 0, stop=kk == 1)
                if g % 2:
                    mm.then_inc(z_done, 1)
            pe.wait_ge(y_pool_ready, 2)
            turn_chunked(TG["pool"], proj[:, 12:14], 4)
            pe.wait_ge(t_free, TG["merged1"] + 2)
            with pe.Fori(0, 2) as i:
                for c in range(2):
                    gemm(At(T0["pool_out"] + c * T_H, 2 * T_H, i), At(G0["pool_out"] + c, 2, i),
                         part(yp_hi), part(yp_lo), T_H)
            with pe.Fori(0, 2) as i:
                for c in range(2):
                    gemm(At(T0["merge_a"] + c * T_K, 2 * T_K, i), At(G0["merge_a"] + c, 2, i), ah, al, T_K)
            with pe.Fori(0, 4) as i:
                gemm(At(T0["merge_b"], 2 * T_K, i), At(G0["merge_b"], 2, i), ah, al, T_K)
                gemm(At(T0["merge_b"] + T_K, 2 * T_K, i), At(G0["merge_b"] + 1, 2, i), part4(y_hi), part4(y_lo), T_K)
            pe.wait_ge(merged_ready, 1)
            turn_chunked(TG["merged1"], ya, 8)
            pe.wait_ge(t_free, TG["norm2"] + 2)
            with pe.Fori(0, 2) as i:
                for c in range(2):
                    gemm(At(T0["out1"] + c * T_K, 2 * T_K, i), At(G0["out1"] + c, 2, i), ah, al, T_K)

            pe.wait_ge(norm_x, 4)
            turn_chunked(TG["norm2"], xn, 8)
            pe.wait_ge(t_free, TG["gqa"] + 2)
            with pe.Fori(0, C_IN2 // 2) as i:
                for c in range(2):
                    gemm(At(T0["proj2"] + c * T_K, 2 * T_K, i), At(G0["proj2"] + c, 2, i), ah, al, T_K)
            gemm(At(T0["proj2"] + (C_IN2 - 1) * T_K), At(G0["proj2"] + C_IN2 - 1), ah, al, T_K)
            pe.wait_ge(proj_in, 1)
            for a in (gqa, na):
                for g in range(2):
                    attention(a, g, At(g), At(TG[a.kind] + g * a.tg))
                pe.wait_ge(a.y_done, TB * a.groups + 1)
            with pe.Fori(0, 4) as i:
                k = At(T0["merge2"], 2 * T_K + 2 * T_H, i)
                g = At(G0["merge2"], 4, i)
                gemm(k, g, ah, al, T_K)
                gemm(k + T_K, g + 1, ah, al, T_K)
                gemm(k + 2 * T_K, g + 2, part4(ya_hi), part4(ya_lo), T_H)
                gemm(k + (2 * T_K + T_H), g + 3, part4(yb_hi), part4(yb_lo), T_H)
            pe.wait_ge(merged_ready, 2)
            turn_chunked(TG["merged2"], ya, 8)
            pe.wait_ge(t_free, TG["norm3"] + 2)
            with pe.Fori(0, 2) as i:
                for c in range(2):
                    gemm(At(T0["out2"] + c * T_K, 2 * T_K, i), At(G0["out2"] + c, 2, i), ah, al, T_K)
            pe.wait_ge(norm_x, 6)
            turn_chunked(TG["norm3"], xn, 8)
            pe.wait_ge(t_free, TG["ff"] + 2)

            def turn_act(j):
                pe.wait_ge(act_ready, j + 1)
                for r in range(2):
                    tr = At(TG["ff"] + r, 2, j) if not isinstance(j, int) else At(TG["ff"] + r + 2 * j)
                    ins = turn(tr, [f_act[:, tb, (2 * r + k) * P:(2 * r + k + 1) * P] for k in range(2) for tb in range(TB)])
                    ins.then_inc(t_done, 1)

            def down(k, g):
                for c in range(4):
                    gemm(k + c * T_Q, g + c, part(f_hi), part(f_lo), T_Q)

            gemm(At(T0["ff_first"]), At(G0["ff_first"]), ah, al, T_K)
            gemm(At(T0["ff_first"] + T_K), At(G0["ff_first"] + 1), ah, al, T_K)
            turn_act(0)
            with pe.Fori(1, FC) as j:
                per = 2 * T_K + 4 * T_Q
                k = At(T0["ff"] - per, per, j)
                g = At(G0["ff"] - 6, 6, j)
                gemm(k, g, ah, al, T_K)
                gemm(k + T_K, g + 1, ah, al, T_K)
                pe.wait_ge(t_free, (At(TG["ff"], 2, j) + 2).n)
                down(k + 2 * T_K, g + 2)
                turn_act(j)
            pe.wait_ge(t_free, TG["ff"] + 2 * FC + 2)
            down(At(T0["ff_last"]), At(G0["ff_last"]))


def tiles(w):
    k, n = w.shape
    return w.reshape(k // 256, 2, P, n // NC, NC).transpose(3, 0, 2, 1, 4).reshape(-1, P, TW)


def columns(v):
    return np.ascontiguousarray(v.reshape(-1, P).T)


def constants():
    f = np.float32
    pos = np.arange(S, dtype=f)
    inv = f(10000.0) ** (-np.arange(HALF, dtype=f) / f(HALF))

    def by_token(cos_sin):
        return np.ascontiguousarray(np.stack(cos_sin).reshape(2, TB, P, HALF).transpose(2, 0, 1, 3)).astype(f)

    ang = pos[:, None] * inv[None]
    inv2 = f(10000.0) ** (-np.arange(0, HALF, 2, dtype=f) / f(HALF))
    row, col = (pos // GRID_W).astype(f), (pos % GRID_W).astype(f)
    ang2 = np.concatenate([row[:, None] * inv2[None], col[:, None] * inv2[None]], axis=-1)
    cpos = (np.arange(N_CMP) * CMP_STRIDE + CMP_BLOCK - 1).astype(f)
    angc = cpos[:, None] * inv[None]
    t = np.arange(S)
    valid = (cpos[None, :] <= t[:, None]).reshape(TB, P, N_CMP).transpose(1, 0, 2)
    causal = np.where(np.arange(P)[None, :] <= np.arange(P)[:, None], 0.0, NEG).astype(f)
    band = np.zeros((P, len(WINDOWS), TB, S), f)
    for g, w in enumerate(WINDOWS):
        m = (t[:, None] <= t[None, :]) & (t[:, None] > t[None, :] - w)
        m = m.astype(f) / np.minimum(t + 1, w).astype(f)[None, :] - np.eye(S, dtype=f)
        band[:, g] = m.reshape(TB, P, S).transpose(1, 0, 2)
    return {
        "ident": np.eye(P, dtype=f), "trig1": by_token((np.cos(ang), np.sin(ang))),
        "trig2": by_token((np.cos(ang2), np.sin(ang2))),
        "trigc": np.ascontiguousarray(np.stack([np.cos(angc), np.sin(angc)], 1)).astype(f),
        "causal": causal, "cmask": np.where(valid, 0.0, NEG).astype(f), "cvalid": valid.astype(f), "band": band,
    }


def layout(v):
    w_in, w_in2 = v["w_in"][0], v["w_in_2"][0]
    at = {"u": 0, "gp": 1024, "q": 2048, "kc": 4096, "vc": 4608, "ks": 5120, "vs": 5632, "kw": 6144, "vw": 6656,
          "gn": 7168}
    order = [("kc", 512), ("vc", 512), ("ks", 512), ("kw", 512), ("vs", 512), ("vw", 512), ("q", 2048), ("u", 1024),
             ("gp", 1024), ("gn", 2048)]
    proj = np.concatenate([w_in[:, at[n]:at[n] + k] for n, k in order], axis=1)
    gbr = np.zeros((1, P, TW), np.float32)
    gbr[0, :, :KT * 3 * NQ] = w_in[:, 9216:].reshape(KT, P, 3 * NQ).transpose(1, 0, 2).reshape(P, -1)

    def cmp_tiles(w):
        return w[0].reshape(8, 4, HD, CMP_H).transpose(0, 2, 1, 3).reshape(8, P, TW)

    pairs = np.concatenate([np.arange(0, HD, 2), np.arange(1, HD, 2)])
    qk = w_in2[:, :1280].reshape(D, 10, HD)[:, :, pairs].reshape(D, 1280)
    proj2 = np.concatenate([qk, w_in2[:, 1280:4608]], axis=1)
    merge, ffd = v["w_merge"][0], v["w_ffn_down_2"][0]

    def per_chunk(*ws):
        ts = [tiles(w).reshape(w.shape[1] // NC, -1, P, TW) for w in ws]
        return np.concatenate(ts, axis=1).reshape(-1, P, TW)

    gate_up = per_chunk(v["w_ffn_gate_2"][0], v["w_ffn_up_2"][0]).reshape(FC, 2 * T_K, P, TW)
    down = np.stack([tiles(ffd[j * NC:(j + 1) * NC]) for j in range(FC)])
    ff = np.concatenate([gate_up[1:], down[:-1]], axis=1).reshape(-1, P, TW)
    ws = np.concatenate([
        tiles(proj), gbr, cmp_tiles(v["cmp_w1_k"]), cmp_tiles(v["cmp_w1_v"]), tiles(v["w_pool_out"][0]),
        tiles(merge[:, :D]), per_chunk(merge[:, D:], v["w_nsa_out"][0]), tiles(v["w_out"][0]),
        tiles(proj2), per_chunk(w_in2[:, 4608:6656], w_in2[:, 6656:], v["w_oa_2"][0], v["w_ob_2"][0]),
        tiles(v["w_out_2"][0]), gate_up[0], ff, down[-1],
    ])
    assert len(ws) == N_TILES, (len(ws), N_TILES)
    wa = v["w_ada_2"][0].T.reshape(N_ADA, P, 2, TW).transpose(0, 2, 1, 3).reshape(2 * N_ADA, P, TW)
    rpb = v["nat_rpb_2"][0]
    tc, scol = np.arange(GRID_W)[:, None], np.arange(GRID_W)[None, :]
    start = np.clip(tc - NA_COLS // 2, 0, GRID_W - NA_COLS)
    inside = (scol >= start) & (scol < start + NA_COLS)
    rel = np.clip(scol - tc + NA_COLS - 1, 0, 2 * NA_COLS - 2)
    rows = rpb[:, NA_ROWS - ROWS:NA_ROWS + ROWS - 1]
    bias = np.where(inside, rows[:, :, rel], np.float32(NEG))
    out = {
        "x": v["x"][0], "ws": ws, "wa": wa, "rpb": bias.transpose(0, 2, 1, 3).reshape(8, GRID_W, -1),
        "n1T": columns(v["norm_w"][0]), "n1T_2": columns(v["norm1_w_2"][0]), "n2T_2": columns(v["norm2_w_2"][0]),
        "peT": np.stack([v["cmp_pe_k"][0].T, v["cmp_pe_v"][0].T], axis=1),
        "b_adaT": columns(v["b_ada_2"][0]),
        "qkn": np.stack([v["q_norm_w_2"][0][pairs], v["k_norm_w_2"][0][pairs]]),
        "c": v["c_2"][0],
        "w2": np.stack([v[n][0].reshape(2, P, HD) for n in ("cmp_w2_k", "cmp_w2_v")]).transpose(2, 0, 1, 3),
        "mix": v["pool_mix"][0].reshape(4, 2, P, POOL_G).transpose(2, 0, 1, 3),
        "pool_scale": v["pool_scale"][0].reshape(2, NC), "b_merge": v["b_merge"][0].reshape(8, NC),
        "final_norm_w": v["final_norm_w"].reshape(4, NC), "final_w": v["final_w_2"].reshape(4, NC),
    }
    return {**out, **constants()}


def kernel(**inputs):
    import concourse.bacc as bacc
    from concourse.bass_utils import run_bass_kernel_spmd

    arrays = {n: np.ascontiguousarray(a) for n, a in layout({n: np.asarray(a) for n, a in inputs.items()}).items()}
    nc = bacc.Bacc("TRN2", target_bir_lowering=False, num_devices=1)
    t = {n: nc.dram_tensor(n + "_dram", a.shape, F32, kind="ExternalInput").ap() for n, a in arrays.items()}
    t["g_rows"] = nc.dram_tensor("g_rows", [2, D], F32).ap()
    t["out"] = nc.dram_tensor("out_dram", [S, D], F32, kind="ExternalOutput").ap()
    build(nc, t)
    r = run_bass_kernel_spmd(nc, [{n + "_dram": a for n, a in arrays.items()}], core_ids=[0])
    return r.results[0]["out_dram"].reshape(1, S, D)
```

```python
from contextlib import ExitStack, contextmanager

import numpy as np

import concourse.bass as bass
from concourse import mybir

ALU = mybir.AluOpType
ACT = mybir.ActivationFunctionType
AX = mybir.AxisListType
F32 = mybir.dt.float32
F32R = mybir.dt.float32r

P = 128
S = 256
TB = S // P
D = 2048
KT = D // P
NC = 512
TW = 1024
RING = 4
ADA_RING = 3
N_CONSTS = 9
EPS = 1e-6
NEG = -1e30
HD = 128
HALF = HD // 2
SCALE = HD ** -0.5
POOL_W = 1024
WINDOWS = (2, 4, 8, 16)
POOL_G = POOL_W // len(WINDOWS)
NQ, NKV = 16, 4
CMP_BLOCK, CMP_STRIDE = 32, 16
N_CMP = (S - CMP_BLOCK) // CMP_STRIDE + 1
CMP_ROWS = NKV * N_CMP
CMP_H = 2 * HD
GRID_W, NA_ROWS, NA_COLS = 64, 8, 16
ROWS = S // GRID_W
D_FF = -(-(8 * D) // (3 * 256)) * 256
FC = D_FF // NC
N_ADA = 6 * D // P
assert S // 64 <= 16 and S <= 512 and ROWS <= NA_ROWS

C_IN = 18
C_IN2 = 9
T_K = D // 256
T_H = T_K // 2
T_Q = T_K // 4
PHASES = [
    ("proj", C_IN * T_K), ("gbr", 1), ("cmp_k", 8), ("cmp_v", 8), ("gates1", 8 * T_K),
    ("merge1", 4 * (T_H + T_K)), ("out1", 4 * T_K),
    ("proj2", C_IN2 * T_K), ("gates2", 8 * T_K), ("merge2", 4 * 2 * T_H), ("out2", 4 * T_K),
    ("ff_first", 2 * T_K), ("ff", (FC - 1) * (2 * T_K + 4 * T_Q)), ("ff_last", 4 * T_Q),
]
T0, N_TILES = {}, 0
for _name, _n in PHASES:
    T0[_name] = N_TILES
    N_TILES += _n
CHUNKS = [
    ("proj", C_IN), ("gbr", 1), ("cmp_k", 1), ("cmp_v", 1), ("gates1", 8), ("merge1", 8),
    ("out1", 4), ("proj2", C_IN2), ("gates2", 8), ("merge2", 8), ("out2", 4),
    ("ff_first", 2), ("ff", 6 * (FC - 1)), ("ff_last", 4),
]
G0, _g = {}, 0
for _name, _n in CHUNKS:
    G0[_name] = _g
    _g += _n
ADA_TURN = {"proj": (12, C_IN // 2), "gates1": (12, 4), "merge1": (6, 2), "out1": (12, 2)}
ADA0, KEPT0, _a, _k = {}, {}, 0, 0
for _name, (_n, _c) in ADA_TURN.items():
    ADA0[_name], KEPT0[_name] = _a, _k
    _a += _n * _c
    _k += _c
N_KEPT = _k
assert _a == 2 * N_ADA


class At:

    def __init__(self, base, per=0, i=None):
        self.base, self.per, self.i = base, per, i

    def __add__(self, k):
        return At(self.base + k, self.per, self.i)

    @property
    def n(self):
        return self.base if self.i is None else self.per * self.i + self.base

    def slot(self, ring):
        assert self.per % ring == 0
        return self.base % ring

    def lap(self, ring, scale):
        c = (self.base // ring + 1) * scale
        return c if self.i is None else (self.per // ring * scale) * self.i + c


class Count:

    def __init__(self, sem):
        self.sem, self.n, self.local = sem, 0, 0

    def on(self, ins):
        ins.then_inc(self.sem, 1)
        self.n = self.n + 1
        self.local += 1


@contextmanager
def turns(eng, times, count, per):
    start = count.n
    with eng.Fori(0, times) as i:
        count.n, count.local = per * i + start, 0
        yield i
    assert count.local == per, (count.local, per)
    count.n = start + per * times


def build(nc, t):
    ctx = ExitStack()
    with ctx:
        K = 1024
        top = [ctx.enter_context(nc.sbuf_tensor("arena", [P, 212800 // 4], F32))]
        base = nc.sbuf_base - 212800
        base = (base + 31) // 32 * 32
        limit = base + 212700

        def at(name, off, shape, dt=F32):
            size = int(np.prod(shape[1:])) * 4
            assert base + off + size <= limit, (name, off + size)
            return nc.alloc_sbuf_tensor_at(name, shape, dt, offset=base + off)

        def sem(name):
            return ctx.enter_context(nc.semaphore(name))

        raw = at("raw", 0, [P, RING, TW])
        w_hi = at("w_hi", 16 * K, [P, RING, TW], F32R)
        w_lo = at("w_lo", 32 * K, [P, RING, TW], F32R)
        a_hi = at("a_hi", 48 * K, [P, KT, S], F32R)
        a_lo = at("a_lo", 64 * K, [P, KT, S], F32R)
        o = [80 * K]

        def const(name, shape):
            r = at(name, o[0], shape)
            o[0] += (int(np.prod(shape[1:])) * 4 + 31) // 32 * 32
            return r

        ident = const("ident", [P, P])
        trig1 = const("trig1", [P, 2, TB, HALF])
        bias_c = at("bias_c", o[0], [P, NC])
        trig2 = const("trig2", [P, 2, TB, HALF])
        qkn = const("qkn", [P, 2, HD])
        trigc = const("trigc", [N_CMP, 2, HALF])
        causal = const("causal", [P, P])
        cmask = const("cmask", [P, TB, N_CMP])
        cvalid = const("cvalid", [P, TB, N_CMP])
        n1T = const("n1T", [P, KT])
        n1T_2 = const("n1T_2", [P, KT])
        n2T_2 = const("n2T_2", [P, KT])
        peT = const("peT", [P, 2, CMP_BLOCK])
        b_adaT = const("b_adaT", [P, N_ADA])
        mod_part = const("mod_part", [P, 12])
        mod2 = const("mod2", [P, 2 * N_ADA])
        mod = const("mod", [P, N_ADA])
        scale1 = const("scale1", [P, KT])
        scale2 = const("scale2", [P, KT])
        ssq = const("ssq", [P, TB])
        rstd = const("rstd", [P, TB])
        gates = const("gates", [P, TB, 3 * NQ])
        hss = const("hss", [P, TB, 5])
        nmax = const("nmax", [P, 4])
        nms = const("nms", [P, 4])
        den = const("den", [P, 4])
        coef = const("coef", [P, 4])
        cmx = const("cmx", [P, 2])
        cden = const("cden", [P, 2])
        pc = const("pc", [P, 2, 2, N_CMP])
        kcT = const("kcT", [P, CMP_ROWS])
        assert o[0] <= 89 * K, o[0]

        ADA = 89 * K
        ada = at("ada", ADA, [P, ADA_RING, TW])
        cb = at("cb", ADA + 12 * K, [P, D])
        kT2 = at("kT2", ADA, [P, 4, S])
        kr2 = at("kr2", ADA + 4 * K, [P, TB, HD])
        gst2 = at("gst2", ADA + 12 * K, [P, TB, NC])
        na_bias = at("na_bias", ADA + 8 * K, [P, 4, S])
        g12 = at("g12", ADA, [P, 2, 4, NC])
        R = ADA + 20 * K
        proj = at("proj", R, [P, C_IN, TB, NC])
        y_hi = at("y_hi", R + 24 * K, [P, 4, 4, S], F32R)
        y_lo = at("y_lo", R + 56 * K, [P, 4, 4, S], F32R)
        yp_hi = at("yp_hi", R, [P, 8, S], F32R)
        yp_lo = at("yp_lo", R + 8 * K, [P, 8, S], F32R)
        scale_b = at("scale_b", R + 16 * K, [P, 2, NC])
        x1 = at("x1", R + 40 * K, [P, 4, TB, NC])
        ya_hi = at("ya_hi", R, [P, 2, 4, S], F32R)
        yb_hi = at("yb_hi", R + 12 * K, [P, 2, 4, S], F32R)
        ya_lo = at("ya_lo", R + 56 * K, [P, 2, 4, S], F32R)
        yb_lo = at("yb_lo", R + 64 * K, [P, 2, 4, S], F32R)
        f_hi = at("f_hi", R, [P, 4, S], F32R)
        f_lo = at("f_lo", R + 4 * K, [P, 4, S], F32R)
        acc = at("acc", R + 8 * K, [P, 4, TB, NC])
        f_silu = at("f_silu", R + 24 * K, [P, TB, NC])
        f_act = at("f_act", R + 28 * K, [P, TB, NC])
        final_b = at("final_b", R + 32 * K, [P, 4, NC])
        SC = R + 72 * K
        xn = at("xn", SC, [P, 4, TB, NC])
        xt = at("xt", SC + 16 * K, [P, 2, NC])
        x0 = at("x0", R, [P, 4, TB, NC])
        ckT = at("ckT", SC, [P, 2, NKV, S])
        kbf = at("kbf", SC + 8 * K, [P, CMP_BLOCK, CMP_ROWS])
        kb_hi = at("kb_hi", SC + 16 * K, [P, CMP_BLOCK, CMP_ROWS], F32R)
        kb_lo = at("kb_lo", R, [P, CMP_BLOCK, CMP_ROWS], F32R)
        w2 = at("w2", SC + 8 * K, [P, 2, 2, HD])
        kcr = at("kcr", SC + 10 * K, [N_CMP, NKV, HD])
        kct = at("kct", SC + 12 * K, [N_CMP, 4, NKV, HALF])
        hdn = at("hdn", SC + 24 * K, [CMP_ROWS, CMP_H])
        hdnT = at("hdnT", SC + 25 * K, [P, 2, 2, CMP_ROWS])
        prob = at("prob", SC, [P, 2, 4, S])
        rt = at("rt", SC, [P, 4, 4, HALF])
        kr1 = at("kr1", SC + 4 * K, [P, TB, 2, HD])
        pt = at("pt", SC + 8 * K, [P, 2, NC])
        sg = at("sg", SC + 8 * K, [P, TB, NC])
        qT = at("qT", SC + 12 * K, [P, 4, S])
        gT = at("gT", SC + 16 * K, [P, 4, S])
        qr = at("qr", SC + 20 * K, [P, TB, 4, HD])
        pcT = at("pcT", SC + 20 * K, [N_CMP, 2 * P])
        ot = at("ot", SC + 21 * K, [P, 2 * P])
        vg = at("vg", SC + 24 * K, [P, TB, 2, HD])
        vcg = at("vcg", SC + 26 * K, [N_CMP, HD])
        kT1 = at("kT1", R, [P, 2, S])
        gst1 = at("gst1", R + 2 * K, [P, TB, NC])
        vc = at("vc", R + 6 * K, [N_CMP, NKV, HD])
        band = at("band", SC, [P, 4, TB, S])
        mix = at("mix", SC + 8 * K, [P, 4, 2, POOL_G])
        poT = at("poT", SC + 16 * K, [P, 8, S])
        ya = at("ya", SC, [P, 4, TB, NC])
        ga = at("ga", SC + 16 * K, [P, TB, NC])
        gb = at("gb", SC + 20 * K, [P, TB, NC])

        ps = ctx.enter_context(nc.psum_tensor("ps", [P, 8, NC], F32))

        def pair(g):
            k = g.slot(2)
            return ps[:, 2 * k:2 * k + 2, :]

        raw_landed = [sem(f"raw_landed{k}") for k in range(RING)]
        hi_done, lo_done, tile_used = sem("hi_done"), sem("lo_done"), sem("tile_used")
        acc_free = sem("acc_free")
        t_done, t_free = sem("t_done"), sem("t_free")
        ada_landed = [sem(f"ada_landed{k}") for k in range(ADA_RING)]
        ada_used, mod_kept = sem("ada_used"), sem("mod_kept")
        first_in = sem("first_in")
        consts_in, x_in, c_in, c_ready = sem("consts_in"), sem("x_in"), sem("c_in"), sem("c_ready")
        norm_sq, norm_var, norm_std, norm_x = sem("norm_sq"), sem("norm_var"), sem("norm_std"), sem("norm_x")
        rstd_ready = sem("rstd_ready")
        xt_ready, t_hi = sem("xt_ready"), sem("t_hi")
        proj_in = sem("proj_in")
        dve_chain, act_chain = sem("dve_chain"), sem("act_chain")
        ck_ready, kb_sum, kb_hi_done, kb_ready = sem("ck_ready"), sem("kb_sum"), sem("kb_hi_done"), sem("kb_ready")
        hdn_ready, hdnT_done, hdnT_ready, w2_in = sem("hdn_ready"), sem("hdnT_done"), sem("hdnT_ready"), sem("w2_in")
        cmp_done, kc_roped, kcT_done, cmp_ready = sem("cmp_done"), sem("kc_roped"), sem("kcT_done"), sem("cmp_ready")
        band_in, po_done, po_copied, z_done = sem("band_in"), sem("po_done"), sem("po_copied"), sem("z_done")
        gp_silu, y_pool_ready = sem("gp_silu"), sem("y_pool_ready")
        scale_in, x1_in, fin_in = sem("scale_in"), sem("x1_in"), sem("fin_in")
        gate_sum, gates_out, gates_back = sem("gate_sum"), sem("gates_out"), sem("gates_back")
        bias_c_in, gate_used, trig2_in = sem("bias_c_in"), sem("gate_used"), sem("trig2_in")
        merged_ready, x1_ready = sem("merged_ready"), sem("x1_ready")
        mod_ready, g_out, g_in = sem("mod_ready"), sem("g_out"), sem("g_in")
        act_ready = sem("act_ready")
        out_ready, out_done = sem("out_ready"), sem("out_done")
        hss_ready, hstd = sem("hss_ready"), sem("hstd")
        bias_in, bias_used = sem("bias_in"), sem("bias_used")

        class Attention:

            def __init__(self, kind, groups, branches, t_groups):
                self.kind, self.groups, self.br, self.tg = kind, groups, branches, t_groups
                self.q_ready = sem(kind + "_q_ready")
                self.sg_ready = sem(kind + "_sg_ready")
                self.v_ready = sem(kind + "_v_ready")
                self.aux_done = sem(kind + "_aux_done")
                self.aux_free = sem(kind + "_aux_free")
                self.qk_done = sem(kind + "_qk_done")
                self.max_ready = sem(kind + "_max_ready")
                self.exp_done = sem(kind + "_exp_done")
                self.p_ready = sem(kind + "_p_ready")
                self.pv_done = sem(kind + "_pv_done")
                self.o_ready = sem(kind + "_o_ready")
                self.y_hi_done = sem(kind + "_y_hi_done")
                self.y_done = sem(kind + "_y_done")

                self.nh = 4 // branches
                self.units = [(tb, h0) for tb in range(TB) for h0 in range(0, 4, self.nh)]

            def keys(self, tb):
                return P * (tb + 1) if self.kind == "nsa" else S

            def rounds(self, tb):
                if self.kind != "nsa":
                    return [[(0, sb)] for sb in range(TB)]
                return [[(b, 0) for b in range(2)]] if tb == 0 else [[(b, sb) for sb in range(TB)] for b in range(2)]

        nsa = Attention("nsa", NKV, 2, 2 + 2 + 2 * 2 + 2 * 3)
        gqa = Attention("gqa", 2, 1, 2 + 4)
        na = Attention("na", 2, 1, 2 + 2 + 4)
        nsa.fill = (6, 2, 0, 2, 2, 2, 2)
        gqa.fill = (6, 2, 3, 3, 2)
        na.fill = (2, 2, 4, 4, 4)

        TG, n = {}, 0
        for name, k in (("norm1", 8), ("nsa", nsa.tg * nsa.groups), ("pool", 4), ("merged1", 8),
                        ("norm2", 8), ("gqa", gqa.tg * 2), ("na", na.tg * 2), ("merged2", 8),
                        ("norm3", 8), ("ff", 2 * FC)):
            TG[name] = n
            n += k
        TH, n = {}, 0
        for name, k in (("norm1", 8), ("pool", 4), ("merged1", 8), ("norm2", 8), ("merged2", 8), ("norm3", 8),
                        ("ff", 2 * FC)):
            TH[name] = n
            n += k
        XT = {"norm1": 0, "norm2": 8, "norm3": 16}
        CMP_COL = NC - 2 * HD // 8
        CH_NSA = 80

        def score(k, w):
            return ps[:, 2 + k // 2, (k % 2) * S:(k % 2) * S + w]

        class Fill:

            def __init__(self, k, step, chunk):
                self.k, self.step, self.chunk, self.at = k, step, chunk, 0

            def __call__(self, n):
                for _ in range(n):
                    self.step(self.k + self.at)
                    self.at += 1
                    if self.at % T_K == 0:
                        self.chunk(self.at // T_K - 1)

        block = ctx.enter_context(nc.Block())

        @block.sync
        def _(sp):
            ws = t["ws"]
            for k in range(RING):
                sp.dma_start(raw[:, k, :], ws[k]).then_inc(raw_landed[k], 16)
            laps = N_TILES // RING
            with sp.Fori(1, laps) as i:
                for k in range(RING):
                    sp.wait_ge(lo_done, RING * i + (k + 1 - RING))
                    sp.dma_start(raw[:, k, :], ws[RING * i + k]).then_inc(raw_landed[k], 16)
            for tile in range(laps * RING, N_TILES):
                sp.wait_ge(lo_done, tile + 1 - RING)
                sp.dma_start(raw[:, tile % RING, :], ws[tile]).then_inc(raw_landed[tile % RING], 16)
            for tb in range(TB):
                sp.wait_ge(out_ready, tb + 1)
                sp.dma_start(t["out"][tb * P:(tb + 1) * P, :].rearrange("p (c n) -> p c n", c=4),
                             xn[:, :, tb, :]).then_inc(out_done, 16)
            sp.wait_ge(out_done, 32)

        @block.gpsimd
        def _(pool):
            for tb in range(TB):
                pool.dma_start(x0[:, :, tb, :], t["x"][tb * P:(tb + 1) * P, :].rearrange("p (c n) -> p c n", c=4))\
                    .then_inc(x_in, 16)
            for dst, name in ((ident, "ident"), (n1T, "n1T")):
                pool.dma_start(dst[:], t[name]).then_inc(first_in, 16)
            small = [(trig1, "trig1"), (trigc, "trigc"), (causal, "causal"),
                     (cmask, "cmask"), (cvalid, "cvalid"), (n1T_2, "n1T_2"), (n2T_2, "n2T_2"),
                     (peT, "peT"), (b_adaT, "b_adaT")]
            for dst, name in small:
                pool.dma_start(dst[:], t[name]).then_inc(consts_in, 16)
            assert len(small) == N_CONSTS
            pool.dma_start(cb[:], t["c"].partition_broadcast(P)).then_inc(c_in, 16)
            pool.dma_start(bias_c[:], t["b_merge"][0].partition_broadcast(P)).then_inc(bias_c_in, 16)
            wa = t["wa"]

            def load_ada(k):
                pool.wait_ge(ada_used, (k + (1 - ADA_RING)).n)
                pool.dma_start(ada[:, k.slot(ADA_RING), :], wa[k.n]).then_inc(ada_landed[k.slot(ADA_RING)], 16)

            for k in range(ADA_RING):
                pool.dma_start(ada[:, k, :], wa[k]).then_inc(ada_landed[k], 16)
            first = ADA0["gates1"] // ADA_RING
            with pool.Fori(1, first) as i:
                for k in range(ADA_RING):
                    load_ada(At(k, ADA_RING, i))
            pool.wait_ge(kb_ready, 2)
            pool.dma_start(w2[:], t["w2"]).then_inc(w2_in, 16)
            for k in range(ADA_RING):
                load_ada(At(ADA0["gates1"] + k))
            with pool.Fori(0, nsa.groups) as i:
                for k in range(12):
                    load_ada(At(ADA0["gates1"] + ADA_RING + k, 12, i))
                for c in range(2):
                    pool.wait_ge(gate_sum, 2 * i + c + 1)
                    pool.dma_start(bias_c[:], t["b_merge"][2 * i + c + 1].partition_broadcast(P)).then_inc(bias_c_in, 16)
            pool.wait_ge(nsa.y_done, len(nsa.units) * nsa.groups + 1)
            pool.dma_start(band[:], t["band"]).then_inc(band_in, 16)
            pool.dma_start(mix[:], t["mix"]).then_inc(band_in, 16)
            pool.dma_start(scale_b[:], t["pool_scale"].partition_broadcast(P)).then_inc(scale_in, 16)
            pool.wait_ge(bias_c_in, 16 * 9)
            pool.dma_start(trig2[:], t["trig2"]).then_inc(trig2_in, 16)
            pool.dma_start(qkn[:], t["qkn"].partition_broadcast(P)).then_inc(trig2_in, 16)

            def gates_load(b, c, used):
                pool.wait_ge(gate_used, used)
                for w, dst in enumerate((ga, gb)):
                    pool.dma_start(dst[:], t["gates"][b, 2 * c + w]).then_inc(gates_back, 16)

            pool.wait_ge(gates_out, 16 * 9)
            pool.wait_ge(y_pool_ready, 2)
            pool.wait_ge(z_done, 2)
            n = ADA_TURN["merge1"][0] // 2
            for c in range(4):
                gates_load(0, c, c + 1)
                for k in range(n):
                    load_ada(At(ADA0["merge1"] + ADA_RING + n * c + k))
            pool.wait_ge(tile_used, T0["merge1"] + 1)
            for tb in range(TB):
                pool.dma_start(x1[:, :, tb, :], t["x"][tb * P:(tb + 1) * P, :].rearrange("p (c n) -> p c n", c=4))\
                    .then_inc(x1_in, 16)
            with pool.Fori((ADA0["out1"] + ADA_RING) // ADA_RING, 2 * N_ADA // ADA_RING) as i:
                for k in range(ADA_RING):
                    load_ada(At(k, ADA_RING, i))
            pool.wait_ge(tile_used, T0["out1"])
            pool.dma_start(final_b[:], t["final_norm_w"].partition_broadcast(P)).then_inc(fin_in, 16)
            pool.wait_ge(mod_ready, 1)
            for n, part in enumerate((2, 5)):
                pool.dma_start(t["g_rows"][n].rearrange("(k p) -> p k", p=P), mod[:, part * KT:(part + 1) * KT],
                               allow_slow_non_contiguous=True)\
                    .then_inc(g_out, 16)
            for g in range(2):
                for tb in range(TB):
                    u = TB * g + tb
                    if u:
                        pool.wait_ge(bias_used, u)
                    for half in range(2):
                        tr = 2 * tb + half
                        for h in range(4):
                            pool.dma_start(
                                na_bias[64 * half:64 * half + 64, h, :],
                                t["rpb"][4 * g + h, :, (ROWS - 1 - tr) * GRID_W:(2 * ROWS - 1 - tr) * GRID_W])\
                                .then_inc(bias_in, 16)
                    if u == 1:
                        pool.wait_ge(gates_out, 16 * 11)
                        pool.wait_ge(gqa.y_done, len(gqa.units) * gqa.groups + 1)
                        gates_load(1, 0, 5)
            pool.wait_ge(gates_out, 16 * 17)
            for c in range(1, 4):
                gates_load(1, c, 4 + c + 1)
            pool.wait_ge(g_out, 32)
            pool.wait_ge(na.y_done, TB * na.groups + 1)
            pool.dma_start(g12[:], t["g_rows"].rearrange("a (c n) -> a c n", c=4).partition_broadcast(P)).then_inc(g_in, 16)
            pool.wait_ge(tile_used, T0["out2"])
            pool.dma_start(final_b[:], t["final_w"].partition_broadcast(P)).then_inc(fin_in, 16)

        @block.scalar
        def _(act):
            chain = Count(act_chain)

            def link(ins):
                chain.on(ins)
                act.wait_ge(act_chain, chain.n)

            def split(k):
                act.wait_ge(raw_landed[k.slot(RING)], k.lap(RING, 16))
                if not (k.i is None and k.base < RING):
                    act.wait_ge(tile_used, (k + (1 - RING)).n)
                act.activation(w_hi[:, k.slot(RING), :], raw[:, k.slot(RING), :], ACT.Copy).then_inc(hi_done, 1)

            def steps(k, n, last=N_TILES):
                for j in range(n):
                    if (k + j).i is not None or (k + j).base + RING < last:
                        split(k + (j + RING))

            def t_copy(r, dst, src=None):
                act.wait_ge(t_done, (r + 1).n)
                act.activation(dst, ps[:, 4 + r.slot(2), :] if src is None else src, ACT.Copy).then_inc(t_free, 1)

            def stats(n, x):
                act.activation(xn[:, :, 0, :], x[:, :, 0, :], ACT.Square, accum_out=ssq[:, 0:1]).then_inc(norm_sq, 1)
                act.wait_ge(norm_var, n + 1)
                act.activation(rstd[:, :], ssq[:, :], ACT.Sqrt).then_inc(norm_std, 1)

            def norm(n, x):
                stats(n, x)
                act.wait_ge(rstd_ready, n + 1)
                act.activation(xn[:, :, 1, :], x[:, :, 1, :], ACT.Copy, scale=rstd[:, 1:2]).then_inc(norm_x, 1)

            def modulated_hi(name):
                for r in range(8):
                    act.wait_ge(xt_ready, XT[name] + r + 1)
                    act.activation(a_hi[:, 2 * r:2 * r + 2, :], xt[:, r % 2, :], ACT.Copy).then_inc(t_hi, 1)

            def transposed_hi(r0, n, dst):
                for r in range(n):
                    act.wait_ge(t_done, r0 + r + 1)
                    act.activation(dst(r), ps[:, 4 + (r0 + r) % 2, :], ACT.Copy).then_inc(t_hi, 1)

            def attention(a, i, g, tg, k, gc):
                nu = len(a.units)
                u0 = At(g.base * nu, g.per * nu, g.i)
                r = At(tg.base, tg.per, tg.i)
                nsa_, na_ = a.kind == "nsa", a.kind == "na"
                kT = kT1 if nsa_ else kT2

                def merge_gate(c):
                    gn = (At(2 * g.base, 2 * g.per, g.i) if nsa_ else At(8 + gc.n - G0["gates2"])) + c
                    if nsa_:
                        act.wait_ge(gate_sum, (gn + 1).n)
                        link(act.activation(gst1[:], gst1[:], ACT.Sigmoid))
                        act.dma_start(t["gates"][0, 2 * i + c], gst1[:]).then_inc(gates_out, 16)
                    else:
                        act.wait_ge(gates_out, 16 * (gn.n + 1))
                        act.wait_ge(tile_used, (k + (c + 1) * T_K).n)
                        act.activation(gst2[:], pair(At(0)), ACT.Sigmoid).then_inc(acc_free, 1)
                        act.wait_ge(acc_free, (gc + c + 3).n)
                        act.dma_start(t["gates"][1, gn.n - 8], gst2[:]).then_inc(gates_out, 16)

                later = []
                fill = Fill(k, lambda x: split(x + RING),
                            lambda c: later.append(c) if nsa_ or c == 1 else merge_gate(c))
                if nsa_:
                    act.wait_ge(a.pv_done, (u0 + 1).n)
                    act.activation(sg[:], proj[:, 14 + i], ACT.Silu).then_inc(a.sg_ready, 1)
                    for b in range(2):
                        act.activation(vg[:, :, b, :], proj[:, 4 + b, :, bass.ds(i * HD, HD)], ACT.Copy)
                    act.activation(vcg[:], vc[:, i, :], ACT.Copy).then_inc(a.v_ready, 1)
                if a.kind == "gqa":
                    for w in range(2):
                        act.wait_ge(hss_ready, 2 * i + w + 1)
                        act.activation(hss[:, :, 4 * w:4 * w + (1 if w else 4)], hss[:, :, 4 * w:4 * w + (1 if w else 4)],
                                       ACT.Sqrt).then_inc(hstd, 1)
                        fill(a.fill[0] // 2)
                else:
                    fill(a.fill[0])
                for h in range(2):
                    t_copy(r, qT[:, 2 * h:2 * h + 2, :])
                    r = r + 1
                if na_:
                    for h in range(2):
                        t_copy(r, kT[:, 2 * h:2 * h + 2, :])
                        r = r + 1
                else:
                    act.wait_ge(a.aux_done, (g + 1).n)
                    act.activation(kT[:, 0:a.br, :], ps[:, 7, 0:a.br * S], ACT.Copy).then_inc(a.aux_free, 1)
                if nsa_:
                    for h in range(2):
                        t_copy(r, gT[:, 2 * h:2 * h + 2, :])
                        r = r + 1
                fill(a.fill[1])
                for j in range(nu + 1):
                    if j < nu:
                        w = a.keys(a.units[j][0])
                        act.wait_ge(a.max_ready, (u0 + j + 1).n)
                        for row in range(4):
                            e = act.activation(prob[:, j % 2, row, 0:w], score(row, w), ACT.Exp,
                                               bias=nms[:, row:row + 1], scale=1.0 if na_ else SCALE,
                                               accum_out=den[:, row:row + 1])
                        if nsa_:
                            e = act.activation(pc[:, j % 2], pc[:, j % 2], ACT.Exp, scale=SCALE)
                        chain.on(e)
                        act.wait_ge(act_chain, chain.n)
                        act.sem_inc(a.exp_done, 1)
                    early = min(a.fill[2 + j], 1)
                    fill(early)
                    if j:
                        if nsa_:
                            t_copy(r, pcT[:], ps[0:N_CMP, 4 + r.slot(2), 0:2 * P])
                            r = r + 1
                        t_copy(r, pt[:, 0, :])
                        r = r + 1
                    fill(a.fill[2 + j] - early)
                    if j:
                        tb, h0 = a.units[j - 1]
                        for n in range(1, len(a.rounds(tb))):
                            t_copy(r, pt[:, n % 2, :])
                            r = r + 1
                        if nsa_:
                            act.wait_ge(a.o_ready, (u0 + j).n)
                            act.activation(y_hi[:, i, h0:h0 + 2, tb * P:(tb + 1) * P],
                                           ot[:].rearrange("p (h s) -> p h s", h=2), ACT.Copy)\
                                .then_inc(a.y_hi_done, 1)
                        else:
                            act.wait_ge(a.pv_done, (u0 + j + 1).n)
                            dst = yb_hi if na_ else ya_hi
                            act.activation(dst[:, i, :, tb * P:(tb + 1) * P],
                                           ps[:, 6, :].rearrange("p (h s) -> p h s", h=4),
                                           ACT.Copy).then_inc(a.y_hi_done, 1)
                    for c in later:
                        merge_gate(c)
                    later.clear()
                assert fill.at == 2 * T_K
            for a in (nsa, gqa, na):
                act.sem_inc(a.exp_done, 1)
                act.sem_inc(a.y_hi_done, 1)
                act.sem_inc(a.aux_free, 1)
            for k in range(RING):
                split(At(k))
            act.wait_ge(x_in, 32)
            norm(0, x0)
            modulated_hi("norm1")
            act.wait_ge(c_in, 16)
            act.activation(cb[:], cb[:], ACT.Silu).then_inc(c_ready, 1)
            with act.Fori(0, C_IN // 2) as i:
                for c in range(2):
                    k = At(T0["proj"] + c * T_K, 2 * T_K, i)
                    steps(k, T_K)
                    act.activation(proj[:, 2 * i + c], pair(At(G0["proj"] + c, 2, i)), ACT.Copy)\
                        .then_inc(acc_free, 1)
            steps(At(T0["gbr"]), 1)
            act.activation(gates[:], pair(At(G0["gbr"]))[:, :, 0:3 * NQ], ACT.Sigmoid).then_inc(acc_free, 1)
            for r in range(4):
                act.wait_ge(kcT_done, r + 1)
                act.activation(ckT[:, r // 2, 2 * (r % 2):2 * (r % 2) + 2, :], ps[:, 4 + r % 2, :], ACT.Copy)\
                    .then_inc(ck_ready, 1)
            for n, name in enumerate(("cmp_k", "cmp_v")):
                act.wait_ge(kb_sum, n + 1)
                if n:
                    act.wait_ge(tile_used, T0["cmp_v"])
                act.activation(kb_hi[:], kbf[:], ACT.Copy).then_inc(kb_hi_done, 1)
                steps(At(T0[name]), 8)
                act.wait_ge(tile_used, T0[name] + 8)
                act.activation(hdn[:], pair(At(G0[name]))[0:CMP_ROWS, 0, 0:CMP_H], ACT.Silu).then_inc(acc_free, 1)
                act.wait_ge(acc_free, G0[name] + 1 + 2)
                act.sem_inc(hdn_ready, 1)
                act.wait_ge(hdnT_done, n + 1)
                act.activation(hdnT[:, n, :, :], ps[:, 4, 0:2 * CMP_ROWS], ACT.Copy).then_inc(hdnT_ready, 1)
            act.wait_ge(cmp_done, 2)
            act.activation(vc[:], ps[0:N_CMP, 5, :], ACT.Copy).then_inc(cmp_ready, 1)
            act.wait_ge(kcT_done, 5)
            act.activation(kcT[:], ps[:, 7, 0:CMP_ROWS], ACT.Copy).then_inc(cmp_ready, 1)
            act.wait_ge(cmp_ready, 2)

            act.sem_inc(gates_out, 16)
            with turns(act, nsa.groups, chain, len(nsa.units) + 2) as i:
                attention(nsa, i, At(0, 1, i), At(TG["nsa"], nsa.tg, i), At(T0["gates1"], 2 * T_K, i),
                          At(G0["gates1"], 2, i))
            act.wait_ge(gates_out, 16 * 9)

            for c in range(2):
                act.activation(proj[:, 12 + c], proj[:, 12 + c], ACT.Silu).then_inc(gp_silu, 1)
            for r in range(4):
                act.wait_ge(po_done, r + 1)
                act.activation(poT[:, 2 * r:2 * r + 2, :], ps[:, r, :], ACT.Copy).then_inc(po_copied, 1)
            transposed_hi(TG["pool"], 4, lambda r: yp_hi[:, 2 * r:2 * r + 2, :])

            with act.Fori(0, 4) as i:
                steps(At(T0["merge1"], T_H + T_K, i), T_H + T_K)
            transposed_hi(TG["merged1"], 8, lambda r: a_hi[:, 2 * r:2 * r + 2, :])
            with act.Fori(0, 4) as i:
                steps(At(T0["out1"], T_K, i), T_K)

            act.wait_ge(x1_ready, 1)
            stats(1, x1)
            act.wait_ge(x1_ready, 2)
            norm(2, x1)
            modulated_hi("norm2")
            with act.Fori(0, C_IN2) as i:
                steps(At(T0["proj2"], T_K, i), T_K)
            for n, a in enumerate((gqa, gqa, na, na)):
                g = n % 2
                attention(a, g, At(g), At(TG[a.kind] + g * a.tg), At(T0["gates2"] + 2 * T_K * n),
                          At(G0["gates2"] + 2 * n))
            with act.Fori(0, 4) as i:
                steps(At(T0["merge2"], 2 * T_H, i), 2 * T_H)
            transposed_hi(TG["merged2"], 8, lambda r: a_hi[:, 2 * r:2 * r + 2, :])
            with act.Fori(0, 4) as i:
                steps(At(T0["out2"], T_K, i), T_K)
            act.wait_ge(x1_ready, 3)
            norm(3, x1)
            modulated_hi("norm3")

            def gate_up(k, g, j):
                steps(k, T_K)
                act.wait_ge(act_ready, j)
                act.wait_ge(acc_free, (g + 2).n)
                act.activation(f_silu[:], pair(g), ACT.Silu).then_inc(acc_free, 1)
                steps(k + T_K, T_K)

            def act_hi(j):
                for r in range(2):
                    tr = At(TG["ff"] + r, 2, j) if not isinstance(j, int) else At(TG["ff"] + r + 2 * j)
                    act.wait_ge(t_done, (tr + 1).n)
                    act.activation(f_hi[:, 2 * r:2 * r + 2, :], ps[:, 4 + tr.slot(2), :], ACT.Copy).then_inc(t_hi, 1)

            gate_up(At(T0["ff_first"]), At(G0["ff_first"]), 0)
            act_hi(0)
            with act.Fori(1, FC) as j:
                per = 2 * T_K + 4 * T_Q
                gate_up(At(T0["ff"] - per, per, j), At(G0["ff"] - 6, 6, j), j)
                steps(At(T0["ff"] - per + 2 * T_K, per, j), 4 * T_Q)
                act_hi(j)
            steps(At(T0["ff_last"]), 4 * T_Q)
            act.wait_ge(x1_ready, 4)
            stats(4, x1)

        @block.vector
        def _(dve):
            chain = Count(dve_chain)

            def link(ins):
                chain.on(ins)
                dve.wait_ge(dve_chain, chain.n)

            def split(k):
                dve.wait_ge(hi_done, (k + 1).n)
                dve.tensor_tensor(w_lo[:, k.slot(RING), :], raw[:, k.slot(RING), :],
                                  w_hi[:, k.slot(RING), :].bitcast(F32), ALU.subtract).then_inc(lo_done, 1)

            def modulation(k, m):
                dve.wait_ge(ada_landed[k.slot(ADA_RING)], k.lap(ADA_RING, 16))
                a = ada[:, k.slot(ADA_RING), :]
                half = k.base % 2
                assert k.per % 2 == 0
                dve.tensor_tensor_reduce(out=a, in0=a, in1=cb[:, half * TW:(half + 1) * TW], scale=1.0, scalar=0.0,
                                         op0=ALU.mult, op1=ALU.add, accum_out=mod_part[:, m:m + 1])\
                    .then_inc(ada_used, 1)

            def keep_modulation(a, n, kept):
                dve.wait_ge(ada_used, (a + n).n)
                dve.tensor_copy(mod2[:, bass.ds(a.n, n)], mod_part[:, 0:n]).then_inc(mod_kept, 1)
                dve.wait_ge(mod_kept, (kept + 1).n)

            def steps(k, n, a=None, na_=0, m0=0):
                done = 0
                for j in range(n):
                    if (k + j).i is not None or (k + j).base + RING < N_TILES:
                        split(k + (j + RING))
                    while done * n < na_ * (j + 1) and done < na_:
                        modulation(a + done, m0 + done)
                        done += 1
            def stats(n, x):
                link(dve.tensor_tensor_reduce(out=xn[:, :, 1, :], in0=x[:, :, 1, :], in1=x[:, :, 1, :], scale=1.0,
                                              scalar=0.0, op0=ALU.mult, op1=ALU.add, accum_out=ssq[:, 1:2]))
                dve.wait_ge(norm_sq, n + 1)
                dve.tensor_scalar(ssq[:, :], ssq[:, :], 1.0 / D, EPS, ALU.mult, ALU.add).then_inc(norm_var, 1)
                dve.wait_ge(norm_std, n + 1)
                link(dve.reciprocal(rstd[:, :], rstd[:, :]))
                dve.sem_inc(rstd_ready, 1)

            def norm(n, x):
                stats(n, x)
                dve.tensor_scalar(xn[:, :, 0, :], x[:, :, 0, :], rstd[:, 0:1], None, ALU.mult).then_inc(norm_x, 1)

            def modulated_lo(name, scale, shift):
                def scaled(r):
                    dve.wait_ge(t_done, TG[name] + r + 1)
                    if r >= 2:
                        dve.wait_ge(t_hi, TH[name] + r - 1)
                    for k in range(2):
                        chain.on(dve.tensor_scalar(
                            xt[:, r % 2, k * S:(k + 1) * S], ps[:, 4 + (TG[name] + r) % 2, k * S:(k + 1) * S],
                            scale[:, 2 * r + k:2 * r + k + 1], shift(2 * r + k), ALU.mult, ALU.add))
                    dve.wait_ge(dve_chain, chain.n)
                    dve.sem_inc(xt_ready, 1)

                scaled(0)
                for r in range(8):
                    if r < 7:
                        scaled(r + 1)
                    dve.wait_ge(t_hi, TH[name] + r + 1)
                    dve.tensor_tensor(a_lo[:, 2 * r:2 * r + 2, :], xt[:, r % 2, :],
                                      a_hi[:, 2 * r:2 * r + 2, :].bitcast(F32), ALU.subtract).then_inc(t_free, 1)

            def transposed_lo(r0, h0, n, hi, lo):
                for r in range(n):
                    dve.wait_ge(t_hi, h0 + r + 1)
                    dve.tensor_tensor(lo(r), ps[:, 4 + (r0 + r) % 2, :], hi(r).bitcast(F32), ALU.subtract)\
                        .then_inc(t_free, 1)

            def rope(src, dst, tmp, trig, bcast):
                cos, sin = bcast(trig, 0), bcast(trig, 1)
                for n, (s, tr) in enumerate(((src[0], cos), (src[1], sin), (src[1], cos), (src[0], sin))):
                    chain.on(dve.tensor_tensor(tmp[n], s, tr, ALU.mult))
                dve.wait_ge(dve_chain, chain.n)
                chain.on(dve.tensor_tensor(dst[0], tmp[0], tmp[1], ALU.subtract))
                chain.on(dve.tensor_tensor(dst[1], tmp[2], tmp[3], ALU.add))
                dve.wait_ge(dve_chain, chain.n)

            def heads(x, h):
                return x[:, :, 0:h, 0:HALF], x[:, :, 0:h, HALF:HD]

            def attention(a, i, g, k, gc, ada0=None, kept=None):
                nu = len(a.units)
                u0 = At(g.base * nu, g.per * nu, g.i)
                nsa_, na_ = a.kind == "nsa", a.kind == "na"
                n_ada = ADA_TURN["gates1"][0]

                def merge_gate(c):
                    if nsa_:
                        gn = At(2 * g.base, 2 * g.per, g.i) + c
                        dve.wait_ge(gates_out, 16 * gn.n + 16)
                        dve.wait_ge(bias_c_in, 16 * gn.n + 16)
                        dve.wait_ge(tile_used, (k + (c + 1) * T_K).n)
                        dve.tensor_tensor(gst1[:], pair(At(0)), bias_c[:].unsqueeze(1).to_broadcast([P, TB, NC]), ALU.add)\
                            .then_inc(acc_free, 1)
                        dve.wait_ge(acc_free, (gc + c + 3).n)
                        dve.sem_inc(gate_sum, 1)

                fill = Fill(k, lambda x: split(x + RING), merge_gate)
                if na_:
                    fill(a.fill[0])
                else:
                    dve.wait_ge(a.pv_done, (u0 + 1).n)
                    dve.wait_ge(a.y_hi_done, (u0 + 1).n)
                    trig = trig1 if nsa_ else trig2

                    def rope_q(src):
                        for tb in range(TB):
                            rope((src[:, tb, :, 0:HALF], src[:, tb, :, HALF:HD]),
                                 (qr[:, tb, :, 0:HALF], qr[:, tb, :, HALF:HD]), [rt[:, n] for n in range(4)], trig,
                                 lambda tr, which: tr[:, which, tb].unsqueeze(1).to_broadcast([P, 4, HALF]))

                    def rope_k(src, dst):
                        rope((src[:, :, 0:HALF], src[:, :, HALF:HD]), (dst[:, :, 0:HALF], dst[:, :, HALF:HD]),
                             [rt[:, n, 0:TB, :] for n in range(4)], trig, lambda tr, which: tr[:, which])

                    if nsa_:
                        rope_q(proj[:, 6 + i].rearrange("p t (h d) -> p t h d", h=4))
                        fill(a.fill[0] // 2)
                        for b in range(2):
                            rope_k(proj[:, 2 + b, :, bass.ds(i * HD, HD)], kr1[:, :, b, :])
                        dve.sem_inc(a.q_ready, 1)
                        fill(a.fill[0] // 2)
                    else:
                        q = proj[:, i].rearrange("p t (h d) -> p t h d", h=4)
                        k_ = proj[:, 2, :, i * HD:(i + 1) * HD]
                        for w, (x, dst, n) in enumerate(((q, qr[:], 4), (k_.unsqueeze(2), kr2[:].unsqueeze(2), 1))):
                            s = hss[:, :, 4 * w:4 * w + n]
                            link(dve.tensor_tensor(dst, x, x, ALU.mult))
                            link(dve.tensor_reduce(s, dst, AX.X, ALU.add))
                            dve.tensor_scalar(s, s, 1.0 / HD, EPS, ALU.mult, ALU.add).then_inc(hss_ready, 1)
                            dve.wait_ge(hstd, 2 * i + w + 1)
                            link(dve.reciprocal(s, s))
                            link(dve.tensor_tensor(dst, x, s.unsqueeze(3).to_broadcast([P, TB, n, HD]), ALU.mult))
                            link(dve.tensor_tensor(dst, dst, qkn[:, w].unsqueeze(1).unsqueeze(1)
                                                   .to_broadcast([P, TB, n, HD]), ALU.mult))
                            if w == 0:
                                rope_q(qr)
                            else:
                                rope_k(kr2, kr2)
                                dve.sem_inc(a.q_ready, 1)
                            fill(a.fill[0] // 2)
                fill(a.fill[1])
                for j in range(nu + 1):
                    if j < nu:
                        u = u0 + j
                        tb, h0 = a.units[j]
                        w = a.keys(tb)
                        sc = ps[:, 2:4, :].rearrange("p b (k s) -> p (b k) s", s=S)
                        pcj = pc[:, j % 2]
                        dve.wait_ge(a.qk_done, (u + 1).n)
                        if nsa_:
                            diag = sc[:, :, w - P:w]
                            chain.on(dve.tensor_tensor(diag, diag, causal[:].unsqueeze(1).to_broadcast([P, 4, P]), ALU.add))
                            small = ps[:, 7, CMP_COL:CMP_COL + 2 * N_CMP].rearrange("p (h n) -> p h n", h=2)
                            chain.on(dve.tensor_tensor(pcj, small, cmask[:, tb].unsqueeze(1).to_broadcast([P, 2, N_CMP]),
                                                       ALU.add))
                            dve.wait_ge(dve_chain, chain.n)
                            chain.on(dve.tensor_reduce(cmx[:], pcj, AX.X, ALU.max))
                        if na_:
                            dve.wait_ge(bias_in, (u + 1).n * 16 * 8)
                            link(dve.scalar_tensor_tensor(out=sc, in0=sc, scalar=SCALE, in1=na_bias[:],
                                                          op0=ALU.mult, op1=ALU.add))
                        chain.on(dve.tensor_reduce(nmax[:], sc[:, :, 0:w], AX.X, ALU.max))
                        dve.wait_ge(dve_chain, chain.n)
                        if na_:
                            dve.sem_inc(bias_used, 1)
                        if nsa_:
                            chain.on(dve.tensor_tensor(pcj, pcj, cmx[:].unsqueeze(2).to_broadcast([P, 2, N_CMP]),
                                                       ALU.subtract))
                        chain.on(dve.tensor_scalar(nms[:], nmax[:], -1.0 if na_ else -SCALE, None, ALU.mult))
                        dve.wait_ge(dve_chain, chain.n)
                        dve.sem_inc(a.max_ready, 1)
                        if nsa_:
                            for m in range(j * n_ada // nu, (j + 1) * n_ada // nu):
                                modulation(ada0 + m, m)
                        dve.wait_ge(a.exp_done, (u + 1 + 1).n)
                        link(dve.reciprocal(den[:], den[:]))
                        if nsa_:
                            chain.on(dve.tensor_reduce(cden[:], pcj, AX.X, ALU.add))
                            gate = gates[:, tb, bass.ds(12 * i + 3 * h0, 6)].rearrange("p (h b) -> p h b", b=3)
                            chain.on(dve.tensor_tensor(coef[:].rearrange("p (h b) -> p h b", b=2),
                                                       den[:].rearrange("p (h b) -> p h b", b=2), gate[:, :, 1:3],
                                                       ALU.mult))
                            dve.wait_ge(dve_chain, chain.n)
                            link(dve.reciprocal(cden[:], cden[:]))
                            link(dve.tensor_tensor(cden[:], cden[:], gate[:, :, 0], ALU.mult))
                            link(dve.tensor_tensor(pcj, pcj, cvalid[:, tb].unsqueeze(1).to_broadcast([P, 2, N_CMP]),
                                                   ALU.mult))
                            chain.on(dve.tensor_tensor(pcj, pcj, cden[:].unsqueeze(2).to_broadcast([P, 2, N_CMP]),
                                                       ALU.mult))
                        cf = coef if nsa_ else den
                        pj = prob[:, j % 2, :, 0:w]
                        chain.on(dve.tensor_tensor(pj, pj, cf[:].unsqueeze(2).to_broadcast([P, 4, w]), ALU.mult))
                        dve.wait_ge(dve_chain, chain.n)
                        dve.sem_inc(a.p_ready, 1)
                    fill(a.fill[2 + j])
                    if j:
                        u = u0 + (j - 1)
                        tb, h0 = a.units[j - 1]
                        o = ps[:, 6, 0:a.nh * P].rearrange("p (h s) -> p h s", h=a.nh)
                        dst = {"nsa": (y_hi, y_lo), "gqa": (ya_hi, ya_lo), "na": (yb_hi, yb_lo)}[a.kind]
                        hi, lo = (d[:, i, h0:h0 + a.nh, tb * P:(tb + 1) * P] for d in dst)
                        if nsa_:
                            dve.wait_ge(a.pv_done, (u + 1 + 1).n)
                            gated = ot[:].rearrange("p (h s) -> p h s", h=2)
                            dve.tensor_tensor(gated, o, gT[:, h0:h0 + 2, tb * P:(tb + 1) * P], ALU.mult)\
                                .then_inc(a.o_ready, 1)
                            o = gated
                        dve.wait_ge(a.y_hi_done, (u + 1 + 1).n)
                        dve.tensor_tensor(lo, o, hi.bitcast(F32), ALU.subtract).then_inc(a.y_done, 1)
                assert fill.at == 2 * T_K
                if nsa_:
                    keep_modulation(ada0, n_ada, kept)
            for a in (nsa, gqa, na):
                dve.sem_inc(a.y_done, 1)
            dve.sem_inc(gate_used, 1)
            dve.memset(nmax[:, :], 0.0).then_inc(acc_free, 2)
            dve.memset(cmx[:, :], 0.0).then_inc(t_free, 2)
            for k in range(RING):
                split(At(k))
            dve.wait_ge(x_in, 32)
            norm(0, x0)
            dve.wait_ge(first_in, 32)
            modulated_lo("norm1", n1T, lambda k: 0.0)
            dve.wait_ge(consts_in, 16 * N_CONSTS)
            dve.wait_ge(c_ready, 1)
            with dve.Fori(0, C_IN // 2) as i:
                n = ADA_TURN["proj"][0]
                steps(At(T0["proj"], 2 * T_K, i), 2 * T_K, At(ADA0["proj"], n, i), n)
                keep_modulation(At(ADA0["proj"], n, i), n, At(KEPT0["proj"], 1, i))
            steps(At(T0["gbr"]), 1)
            dve.wait_ge(ck_ready, 4)
            for n, name in enumerate(("cmp_k", "cmp_v")):
                if n:
                    dve.wait_ge(kb_hi_done, 1)
                for half in range(2):
                    src = ckT[:, n].rearrange("p h (m l) -> p h m l", l=CMP_STRIDE)[:, :, half:half + N_CMP, :]
                    ls = slice(half * CMP_STRIDE, (half + 1) * CMP_STRIDE)
                    dst = kbf[:, ls, :].rearrange("p l (h m) -> p h m l", h=NKV)
                    for h in range(NKV):
                        ins = dve.tensor_tensor(dst[:, h], src[:, h],
                                                peT[:, n, ls].unsqueeze(1).to_broadcast([P, N_CMP, CMP_STRIDE]), ALU.add)
                        chain.on(ins)
                dve.wait_ge(dve_chain, chain.n)
                dve.sem_inc(kb_sum, 1)
                dve.wait_ge(kb_hi_done, n + 1)
                dve.tensor_tensor(kb_lo[:], kbf[:], kb_hi[:].bitcast(F32), ALU.subtract).then_inc(kb_ready, 1)
                steps(At(T0[name]), 8)
            dve.wait_ge(cmp_done, 1)
            link(dve.tensor_copy(kcr[:], ps[0:N_CMP, 6, :].rearrange("p (h d) -> p h d", h=NKV)))
            rope((kcr[:, :, 0:HALF], kcr[:, :, HALF:HD]), (kcr[:, :, 0:HALF], kcr[:, :, HALF:HD]),
                 [kct[:, n] for n in range(4)], trigc,
                 lambda tr, which: tr[:, which].unsqueeze(1).to_broadcast([N_CMP, NKV, HALF]))
            dve.sem_inc(kc_roped, 1)

            with turns(dve, nsa.groups, chain, CH_NSA) as i:
                attention(nsa, i, At(0, 1, i), At(T0["gates1"], 2 * T_K, i), At(G0["gates1"], 2, i),
                          At(ADA0["gates1"], ADA_TURN["gates1"][0], i), At(KEPT0["gates1"], 1, i))

            dve.wait_ge(gp_silu, 2)
            dve.wait_ge(scale_in, 16)
            for c in range(2):
                g = proj[:, 12 + c]
                chain.on(dve.tensor_tensor(g, g, scale_b[:, c].unsqueeze(1).to_broadcast([P, TB, NC]), ALU.mult))
            for c in range(2):
                dve.wait_ge(z_done, c + 1)
                dve.wait_ge(dve_chain, chain.n)
                g = proj[:, 12 + c]
                dve.tensor_tensor(g, ps[:, 2 * c:2 * c + 2, :], g, ALU.mult).then_inc(y_pool_ready, 1)
            transposed_lo(TG["pool"], TH["pool"], 4, lambda r: yp_hi[:, 2 * r:2 * r + 2, :],
                          lambda r: yp_lo[:, 2 * r:2 * r + 2, :])

            def merge(blk, c, k, g, n_b, ada=lambda part: ()):
                steps(k, T_H, *ada(0))
                dve.wait_ge(gates_back, 32 * c + 32 * (4 * blk + 1))
                dve.wait_ge(tile_used, (k + T_H).n)
                dve.tensor_tensor(ga[:], pair(g), ga[:], ALU.mult).then_inc(acc_free, 1)
                steps(k + T_H, n_b, *ada(1))
                dve.wait_ge(tile_used, (k + (T_H + n_b)).n)
                dve.tensor_tensor(gb[:], pair(g + 1), gb[:], ALU.mult).then_inc(acc_free, 1)
                dve.wait_ge(acc_free, (g + 4).n)
                link(dve.tensor_tensor(ya[:, c], ga[:], gb[:], ALU.add))
                dve.sem_inc(gate_used, 1)

            with turns(dve, 2, chain, 2) as i:
                n = ADA_TURN["merge1"][0]
                per = T_H + T_K
                for c in range(2):
                    def ada_part(part, c=c):
                        m0 = c * n // 2 + part * (n // 6)
                        return At(ADA0["merge1"] + m0, n, i), (n // 6, n // 3)[part], m0

                    merge(0, 2 * i + c, At(T0["merge1"] + c * per, 2 * per, i), At(G0["merge1"] + 2 * c, 4, i), T_K,
                          ada_part)
                keep_modulation(At(ADA0["merge1"], n, i), n, At(KEPT0["merge1"], 1, i))
            dve.sem_inc(merged_ready, 1)
            transposed_lo(TG["merged1"], TH["merged1"], 8, lambda r: a_hi[:, 2 * r:2 * r + 2, :],
                          lambda r: a_lo[:, 2 * r:2 * r + 2, :])
            dve.wait_ge(x1_in, 32)
            with dve.Fori(0, 2) as i:
                for c in range(2):
                    k = At(T0["out1"] + c * T_K, 2 * T_K, i)
                    n = ADA_TURN["out1"][0]
                    steps(k, T_K, At(ADA0["out1"] + c * n // 2, n, i), n // 2, c * n // 2)
                    dve.wait_ge(tile_used, (k + T_K).n)
                    x = x1[:, 2 * i + c]
                    dve.tensor_tensor(x, pair(At(G0["out1"] + c, 2, i)), x, ALU.add).then_inc(acc_free, 1)
                keep_modulation(At(ADA0["out1"], n, i), n, At(KEPT0["out1"], 1, i))
            dve.wait_ge(acc_free, G0["out1"] + 4 + 2)
            dve.sem_inc(x1_ready, 1)
            stats(1, x1)
            dve.wait_ge(fin_in, 16)
            for tb in range(TB):
                chain.on(dve.scalar_tensor_tensor(out=x1[:, :, tb, :], in0=x1[:, :, tb, :], scalar=rstd[:, tb:tb + 1],
                                                  in1=final_b[:], op0=ALU.mult, op1=ALU.mult))
            dve.wait_ge(dve_chain, chain.n)
            dve.sem_inc(x1_ready, 1)
            dve.wait_ge(mod_kept, N_KEPT)
            link(dve.tensor_tensor(mod[:], mod2[:].rearrange("p (n h) -> p n h", h=2)[:, :, 0],
                                   mod2[:].rearrange("p (n h) -> p n h", h=2)[:, :, 1], ALU.add))
            link(dve.tensor_tensor(mod[:], mod[:], b_adaT[:], ALU.add))
            dve.sem_inc(mod_ready, 1)
            chain.on(dve.scalar_tensor_tensor(out=scale1[:], in0=mod[:, KT:2 * KT], scalar=1.0, in1=n1T_2[:],
                                              op0=ALU.add, op1=ALU.mult))
            chain.on(dve.scalar_tensor_tensor(out=scale2[:], in0=mod[:, 4 * KT:5 * KT], scalar=1.0, in1=n2T_2[:],
                                              op0=ALU.add, op1=ALU.mult))
            dve.wait_ge(dve_chain, chain.n)
            norm(2, x1)
            modulated_lo("norm2", scale1, lambda k: mod[:, k:k + 1])

            def copy_out(c, k, g):
                dve.wait_ge(tile_used, (k + T_K).n)
                dve.tensor_copy(proj[:, c], pair(g)).then_inc(acc_free, 1)

            with dve.Fori(0, C_IN2 // 2) as i:
                for c in range(2):
                    k = At(T0["proj2"] + c * T_K, 2 * T_K, i)
                    steps(k, T_K)
                    copy_out(2 * i + c, k, At(G0["proj2"] + c, 2, i))
            k = At(T0["proj2"] + (C_IN2 - 1) * T_K)
            steps(k, T_K)
            copy_out(C_IN2 - 1, k, At(G0["proj2"] + C_IN2 - 1))
            dve.wait_ge(acc_free, G0["gates2"] + 2)
            dve.sem_inc(proj_in, 1)
            dve.wait_ge(trig2_in, 32)
            for n, a in enumerate((gqa, gqa, na, na)):
                attention(a, n % 2, At(n % 2), At(T0["gates2"] + 2 * T_K * n), At(G0["gates2"] + 2 * n))

            with turns(dve, 4, chain, 1) as i:
                merge(1, i, At(T0["merge2"], 2 * T_H, i), At(G0["merge2"], 2, i), T_H)
            dve.wait_ge(dve_chain, chain.n)
            dve.sem_inc(merged_ready, 1)
            transposed_lo(TG["merged2"], TH["merged2"], 8, lambda r: a_hi[:, 2 * r:2 * r + 2, :],
                          lambda r: a_lo[:, 2 * r:2 * r + 2, :])
            dve.wait_ge(g_in, 16)
            with turns(dve, 2, chain, 2) as i:
                for c in range(2):
                    k = At(T0["out2"] + c * T_K, 2 * T_K, i)
                    g = At(G0["out2"] + c, 2, i)
                    steps(k, T_K)
                    dve.wait_ge(tile_used, (k + T_K).n)
                    ins = dve.tensor_tensor(gb[:], pair(g), g12[:, 0, 2 * i + c, :].unsqueeze(1).to_broadcast([P, TB, NC]),
                                            ALU.mult)
                    ins.then_inc(acc_free, 1)
                    dve.wait_ge(acc_free, (g + 3).n)
                    x = x1[:, 2 * i + c]
                    link(dve.tensor_tensor(x, x, gb[:], ALU.add))
            dve.sem_inc(x1_ready, 1)
            norm(3, x1)
            modulated_lo("norm3", scale2, lambda k: mod[:, 3 * KT + k:3 * KT + k + 1])
            link(dve.memset(acc[:], 0.0))

            def gate_up(k, g, j):
                steps(k, 2 * T_K)
                dve.wait_ge(acc_free, (g + 3).n)
                dve.wait_ge(tile_used, (k + 2 * T_K).n)
                dve.tensor_tensor(f_act[:], pair(g + 1), f_silu[:], ALU.mult).then_inc(acc_free, 1)
                dve.wait_ge(acc_free, (g + 4).n)
                dve.sem_inc(act_ready, 1)

            def down(k, g):
                for c in range(4):
                    steps(k + c * T_Q, T_Q)
                    dve.wait_ge(tile_used, (k + (c + 1) * T_Q).n)
                    dve.tensor_tensor(acc[:, c], pair(g + c), acc[:, c], ALU.add).then_inc(acc_free, 1)

            def act_lo(j):
                for r in range(2):
                    tr = At(TG["ff"] + r, 2, j) if not isinstance(j, int) else At(TG["ff"] + r + 2 * j)
                    h = At(TH["ff"] + r, 2, j) if not isinstance(j, int) else At(TH["ff"] + r + 2 * j)
                    dve.wait_ge(t_hi, (h + 1).n)
                    dve.tensor_tensor(f_lo[:, 2 * r:2 * r + 2, :], ps[:, 4 + tr.slot(2), :],
                                      f_hi[:, 2 * r:2 * r + 2, :].bitcast(F32), ALU.subtract).then_inc(t_free, 1)

            gate_up(At(T0["ff_first"]), At(G0["ff_first"]), 0)
            act_lo(0)
            with dve.Fori(1, FC) as j:
                per = 2 * T_K + 4 * T_Q
                gate_up(At(T0["ff"] - per, per, j), At(G0["ff"] - 6, 6, j), j)
                down(At(T0["ff"] - per + 2 * T_K, per, j), At(G0["ff"] - 6 + 2, 6, j))
                act_lo(j)
            dve.wait_ge(fin_in, 32)
            for c in range(4):
                steps(At(T0["ff_last"] + c * T_Q), T_Q)
                dve.wait_ge(tile_used, T0["ff_last"] + (c + 1) * T_Q)
                dve.tensor_tensor(acc[:, c], pair(At(G0["ff_last"] + c)), acc[:, c], ALU.add).then_inc(acc_free, 1)
                dve.wait_ge(acc_free, G0["ff_last"] + c + 3)
                link(dve.tensor_tensor(acc[:, c], acc[:, c], g12[:, 1, c, :].unsqueeze(1).to_broadcast([P, TB, NC]),
                                       ALU.mult))
                link(dve.tensor_tensor(x1[:, c], x1[:, c], acc[:, c], ALU.add))
            dve.sem_inc(x1_ready, 1)
            stats(4, x1)
            for tb in range(TB):
                dve.scalar_tensor_tensor(out=xn[:, :, tb, :], in0=x1[:, :, tb, :], scalar=rstd[:, tb:tb + 1],
                                         in1=final_b[:], op0=ALU.mult, op1=ALU.mult).then_inc(out_ready, 1)

        @block.tensor
        def _(pe):
            def tile(k, out, n, of, hi, lo, kts=2, rows=P, blocks=TB, width=NC):
                pe.wait_ge(lo_done, (k + 1).n)
                s = k.slot(RING)
                for q in range(kts):
                    cols = slice(q * width, (q + 1) * width)
                    m = n * kts + q
                    for tb in range(blocks):
                        o = out[0:rows, tb, 0:width]
                        pe.matmul(o, hi(m, tb), w_hi[:, s, cols], start=m == 0, stop=False)
                        pe.matmul(o, hi(m, tb), w_lo[:, s, cols], start=False, stop=False)
                        mm = pe.matmul(o, lo(m, tb), w_hi[:, s, cols], start=False, stop=m == of * kts - 1)
                mm.then_inc(tile_used, 1)

            def gemm(k, g, hi, lo, tiles, **sizes):
                pe.wait_ge(acc_free, (g + 1).n)
                for j in range(tiles):
                    tile(k + j, pair(g), j, tiles, hi, lo, **sizes)

            def part(x):
                return lambda n, tb: x[:, n, tb * P:(tb + 1) * P]

            def part4(x):
                return lambda n, tb: x[:, n // 4, n % 4, tb * P:(tb + 1) * P]

            def turn(r, blocks, bank=None):
                if bank is None:
                    pe.wait_ge(t_free, (r + 1).n)
                    bank = 4 + r.slot(2)
                for n, b in enumerate(blocks):
                    m = b.shape[-1]
                    ins = pe.transpose(ps[0:m, bank, n * P:n * P + b.shape[0]], b, ident[0:b.shape[0], 0:b.shape[0]])
                return ins

            def turn_chunked(name, x, n, hi, lo):
                r0, nxt = TG[name], name_after[name]
                k, g = At(T0[nxt]), At(G0[nxt])

                def products(j):
                    pe.wait_ge(t_free, r0 + j + 3)
                    tile(k + j, pair(g), j, n, hi, lo)

                pe.wait_ge(acc_free, (g + 1).n)
                for r in range(n):
                    blocks = [x[:, (2 * r + m) // 4, tb, ((2 * r + m) % 4) * P:((2 * r + m) % 4 + 1) * P]
                              for m in range(2) for tb in range(TB)]
                    turn(At(r0 + r), blocks).then_inc(t_done, 1)
                    if 0 <= r - 2 < RING:
                        products(r - 2)
                for j in range(min(n - 2, RING), n):
                    products(j)

            name_after = {"norm1": "proj", "pool": "merge1", "merged1": "out1", "norm2": "proj2",
                          "merged2": "out2", "norm3": "ff_first"}
            ah, al = part(a_hi), part(a_lo)

            def attention(a, i, g, tg, k, gc):
                nu = len(a.units)
                u0 = At(g.base * nu, g.per * nu, g.i)
                r = At(tg.base, tg.per, tg.i)
                nsa_, na_ = a.kind == "nsa", a.kind == "na"
                kT = kT1 if nsa_ else kT2

                def gate_tile(x):
                    c, n = fill.at // T_K, fill.at % T_K
                    if n == 0:
                        pe.wait_ge(acc_free, (gc + c + 2).n)
                    tile(x, pair(At(0)), n, T_K, part(a_hi), part(a_lo))

                fill = Fill(k, gate_tile, lambda c: None)
                fill(a.fill[0])
                if na_:
                    q = proj[:, 3 + i].rearrange("p t (h d) -> p t h d", h=4)
                else:
                    q = qr
                    pe.wait_ge(a.q_ready, (g + 1).n)
                for h in range(2):
                    turn(r, [q[:, tb, 2 * h + m, :] for m in range(2) for tb in range(TB)]).then_inc(t_done, 1)
                    r = r + 1
                if na_:
                    k_ = proj[:, 5 + i].rearrange("p t (h d) -> p t h d", h=4)
                    for h in range(2):
                        turn(r, [k_[:, tb, 2 * h + m, :] for m in range(2) for tb in range(TB)]).then_inc(t_done, 1)
                        r = r + 1
                else:
                    pe.wait_ge(a.aux_free, (g + 1).n)
                    ks = [kr1[:, tb, b, :] for b in range(2) for tb in range(TB)] if nsa_ else \
                        [kr2[:, tb, :] for tb in range(TB)]
                    turn(r, ks, bank=7).then_inc(a.aux_done, 1)
                if nsa_:
                    pe.wait_ge(a.sg_ready, (g + 1).n)
                    for h in range(2):
                        turn(r, [sg[:, tb, (2 * h + m) * HD:(2 * h + m + 1) * HD] for m in range(2) for tb in range(TB)])\
                            .then_inc(t_done, 1)
                        r = r + 1
                fill(a.fill[1])
                if nsa_:
                    pe.wait_ge(a.v_ready, (g + 1).n)
                pe.wait_ge(t_free, (r + 2).n)
                if not na_:
                    pe.wait_ge(a.aux_free, (g + 2).n)
                for j in range(nu + 1):
                    if j < nu:
                        tb, h0 = a.units[j]
                        w = a.keys(tb)
                        pe.wait_ge(a.exp_done, (u0 + j + 1).n)
                        for n, h in enumerate(range(h0, h0 + a.nh)):
                            lhs = qT[:, h, tb * P:(tb + 1) * P]
                            if nsa_:
                                out = ps[:, 2 + n, :].rearrange("p (b s) -> p b s", b=2)[:, :, 0:w]
                                pe.matmul(out, lhs, kT[:, 0:2, 0:w], start=True, stop=True)
                                mm = pe.matmul(ps[:, 7, CMP_COL + n * N_CMP:CMP_COL + (n + 1) * N_CMP], lhs,
                                               kcT[:, bass.ds(i * N_CMP, N_CMP)], start=True, stop=True)
                            else:
                                mm = pe.matmul(score(n, S), lhs, kT[:, h if na_ else 0, :], start=True, stop=True)
                        mm.then_inc(a.qk_done, 1)
                    early = min(a.fill[2 + j], 1)
                    fill(early)
                    if j:
                        u = u0 + (j - 1)
                        tb, h0 = a.units[j - 1]
                        rounds = a.rounds(tb)
                        pr = prob[:, (j - 1) % 2]
                        pe.wait_ge(a.p_ready, (u + 1).n)

                        def transposes(n, r):
                            turn(r + n, [pr[:, h * a.br + b, sb * P:(sb + 1) * P] for b, sb in rounds[n]
                                         for h in range(a.nh)]).then_inc(t_done, 1)

                        if nsa_:
                            turn(r, [pc[:, (j - 1) % 2, h, :] for h in range(2)]).then_inc(t_done, 1)
                            r = r + 1
                        transposes(0, r)
                    fill(a.fill[2 + j] - early)
                    if j:
                        pe.wait_ge(a.y_done, (u + 1).n)
                        if nsa_:
                            pe.wait_ge(t_free, (r + 2).n)
                            pe.matmul(ps[:, 6, 0:2 * P], vcg[:], pcT[:], start=True, stop=False)
                        for n in range(len(rounds)):
                            if n + 1 < len(rounds):
                                transposes(n + 1, r)
                            pe.wait_ge(t_free, (r + (n + 3)).n)
                            last = n == len(rounds) - 1
                            if na_:
                                sb = rounds[n][0][1]
                                for h in range(4):
                                    v = proj[:, 7 + i, sb, h * HD:(h + 1) * HD]
                                    mm = pe.matmul(ps[:, 6, h * P:(h + 1) * P], v, pt[:, n % 2, h * P:(h + 1) * P],
                                                   start=n == 0 and h == 0, stop=last, skip_group_check=True)
                            else:
                                for m, (b, sb) in enumerate(rounds[n]):
                                    v = vg[:, sb, b, :] if nsa_ else proj[:, 2, sb, 256 + i * HD:256 + (i + 1) * HD]
                                    cols = slice(m * a.nh * P, (m + 1) * a.nh * P)
                                    mm = pe.matmul(ps[:, 6, 0:a.nh * P], v, pt[:, n % 2, cols],
                                                   start=n == 0 and not nsa_, stop=last and m == len(rounds[n]) - 1)
                        mm.then_inc(a.pv_done, 1)
                        r = r + len(rounds)
                assert fill.at == 2 * T_K

            for a in (nsa, gqa, na):
                pe.sem_inc(a.pv_done, 1)
            pe.wait_ge(first_in, 32)
            pe.wait_ge(norm_x, 2)
            turn_chunked("norm1", xn, 8, ah, al)
            with pe.Fori(0, C_IN // 2 - 1) as i:
                for c in (1, 2):
                    gemm(At(T0["proj"] + c * T_K, 2 * T_K, i), At(G0["proj"] + c, 2, i), ah, al, T_K)
            gemm(At(T0["proj"] + (C_IN - 1) * T_K), At(G0["proj"] + C_IN - 1), ah, al, T_K)
            gemm(At(T0["gbr"]), At(G0["gbr"]), ah, al, 1, kts=KT, width=3 * NQ)
            pe.wait_ge(acc_free, C_IN + 2)
            for r in range(4):
                if r >= 2:
                    pe.wait_ge(ck_ready, r - 1)
                blocks = [proj[:, r // 2, tb, (2 * (r % 2) + k) * HD:(2 * (r % 2) + k + 1) * HD]
                          for k in range(2) for tb in range(TB)]
                turn(None, blocks, bank=4 + r % 2).then_inc(kcT_done, 1)
            for n, name in enumerate(("cmp_k", "cmp_v")):
                pe.wait_ge(kb_ready, n + 1)
                gemm(At(T0[name]), At(G0[name]), lambda m, tb: kb_hi[:, m, :], lambda m, tb: kb_lo[:, m, :], 8,
                     kts=4, rows=CMP_ROWS, blocks=1, width=CMP_H)
                pe.wait_ge(hdn_ready, n + 1)
                for f in range(2):
                    ins = pe.transpose(ps[:, 4, f * CMP_ROWS:(f + 1) * CMP_ROWS], hdn[:, f * P:(f + 1) * P],
                                       ident[0:CMP_ROWS, 0:CMP_ROWS])
                ins.then_inc(hdnT_done, 1)
                pe.wait_ge(hdnT_ready, n + 1)
            pe.wait_ge(w2_in, 16)
            for n in range(2):
                for h in range(NKV):
                    for f in range(2):
                        mm = pe.matmul(ps[0:N_CMP, 6 - n, h * HD:(h + 1) * HD],
                                       hdnT[:, n, f, h * N_CMP:(h + 1) * N_CMP], w2[:, n, f, :],
                                       start=f == 0, stop=f == 1)
                mm.then_inc(cmp_done, 1)
            pe.wait_ge(kc_roped, 1)
            for h in range(NKV):
                ins = pe.transpose(ps[:, 7, h * N_CMP:(h + 1) * N_CMP], kcr[:, h, :], ident[0:N_CMP, 0:N_CMP])
            ins.then_inc(kcT_done, 1)
            pe.wait_ge(cmp_ready, 2)

            pe.wait_ge(acc_free, G0["gates1"] + 2)
            with pe.Fori(0, nsa.groups) as i:
                attention(nsa, i, At(0, 1, i), At(TG["nsa"], nsa.tg, i), At(T0["gates1"], 2 * T_K, i),
                          At(G0["gates1"], 2, i))
            pe.wait_ge(nsa.y_done, len(nsa.units) * nsa.groups + 1)
            pe.wait_ge(acc_free, G0["merge1"] + 2)

            pe.wait_ge(band_in, 32)
            for ct in range(8):
                for tb in range(TB):
                    mm = pe.matmul(ps[:, ct // 2, (ct % 2) * S:(ct % 2 + 1) * S],
                                   proj[:, 10 + ct // 4, tb, (ct % 4) * P:(ct % 4 + 1) * P],
                                   band[:, ct // 2, tb, :], start=tb == 0, stop=tb == 1)
                if ct % 2:
                    mm.then_inc(po_done, 1)
            pe.wait_ge(po_copied, 4)
            for g in range(4):
                for tb in range(TB):
                    for kk in range(2):
                        mm = pe.matmul(ps[:, 2 * (g // 2) + tb, (g % 2) * POOL_G:(g % 2 + 1) * POOL_G],
                                       poT[:, 2 * g + kk, tb * P:(tb + 1) * P], mix[:, g, kk, :],
                                       start=kk == 0, stop=kk == 1)
                if g % 2:
                    mm.then_inc(z_done, 1)
            pe.wait_ge(y_pool_ready, 2)
            turn_chunked("pool", proj[:, 12:14], 4, part(yp_hi), part(yp_lo))
            gemm(At(T0["merge1"] + T_H), At(G0["merge1"] + 1), part4(y_hi), part4(y_lo), T_K)
            with pe.Fori(1, 4) as i:
                k = At(T0["merge1"], T_H + T_K, i)
                g = At(G0["merge1"], 2, i)
                gemm(k, g, part(yp_hi), part(yp_lo), T_H)
                gemm(k + T_H, g + 1, part4(y_hi), part4(y_lo), T_K)
            pe.wait_ge(merged_ready, 1)
            turn_chunked("merged1", ya, 8, ah, al)
            for c in range(1, 4):
                gemm(At(T0["out1"] + c * T_K), At(G0["out1"] + c), ah, al, T_K)

            pe.wait_ge(norm_x, 4)
            turn_chunked("norm2", xn, 8, ah, al)
            with pe.Fori(0, C_IN2 // 2) as i:
                for c in (1, 2):
                    gemm(At(T0["proj2"] + c * T_K, 2 * T_K, i), At(G0["proj2"] + c, 2, i), ah, al, T_K)
            pe.wait_ge(proj_in, 1)
            for n, a in enumerate((gqa, gqa, na, na)):
                g = n % 2
                attention(a, g, At(g), At(TG[a.kind] + g * a.tg), At(T0["gates2"] + 2 * T_K * n),
                          At(G0["gates2"] + 2 * n))
                if g:
                    pe.wait_ge(a.y_done, len(a.units) * a.groups + 1)
            pe.wait_ge(acc_free, G0["merge2"] + 2)
            with pe.Fori(0, 4) as i:
                k = At(T0["merge2"], 2 * T_H, i)
                g = At(G0["merge2"], 2, i)
                gemm(k, g, part4(ya_hi), part4(ya_lo), T_H)
                gemm(k + T_H, g + 1, part4(yb_hi), part4(yb_lo), T_H)
            pe.wait_ge(merged_ready, 2)
            turn_chunked("merged2", ya, 8, ah, al)
            for c in range(1, 4):
                gemm(At(T0["out2"] + c * T_K), At(G0["out2"] + c), ah, al, T_K)
            pe.wait_ge(norm_x, 6)
            turn_chunked("norm3", xn, 8, ah, al)

            def turn_act(j):
                pe.wait_ge(act_ready, j + 1)
                for r in range(2):
                    tr = At(TG["ff"] + r, 2, j) if not isinstance(j, int) else At(TG["ff"] + r + 2 * j)
                    ins = turn(tr, [f_act[:, tb, (2 * r + k) * P:(2 * r + k + 1) * P] for k in range(2) for tb in range(TB)])
                    ins.then_inc(t_done, 1)

            def down(k, g):
                for c in range(4):
                    gemm(k + c * T_Q, g + c, part(f_hi), part(f_lo), T_Q)

            gemm(At(T0["ff_first"] + T_K), At(G0["ff_first"] + 1), ah, al, T_K)
            turn_act(0)
            with pe.Fori(1, FC) as j:
                per = 2 * T_K + 4 * T_Q
                k = At(T0["ff"] - per, per, j)
                g = At(G0["ff"] - 6, 6, j)
                gemm(k, g, ah, al, T_K)
                gemm(k + T_K, g + 1, ah, al, T_K)
                pe.wait_ge(t_free, (At(TG["ff"], 2, j) + 2).n)
                down(k + 2 * T_K, g + 2)
                turn_act(j)
            pe.wait_ge(t_free, TG["ff"] + 2 * FC + 2)
            down(At(T0["ff_last"]), At(G0["ff_last"]))


def tiles(w):
    k, n = w.shape
    return w.reshape(k // 256, 2, P, n // NC, NC).transpose(3, 0, 2, 1, 4).reshape(-1, P, TW)


def columns(v):
    return np.ascontiguousarray(v.reshape(-1, P).T)


def constants():
    f = np.float32
    pos = np.arange(S, dtype=f)
    inv = f(10000.0) ** (-np.arange(HALF, dtype=f) / f(HALF))

    def by_token(cos_sin):
        return np.ascontiguousarray(np.stack(cos_sin).reshape(2, TB, P, HALF).transpose(2, 0, 1, 3)).astype(f)

    ang = pos[:, None] * inv[None]
    inv2 = f(10000.0) ** (-np.arange(0, HALF, 2, dtype=f) / f(HALF))
    row, col = (pos // GRID_W).astype(f), (pos % GRID_W).astype(f)
    ang2 = np.concatenate([row[:, None] * inv2[None], col[:, None] * inv2[None]], axis=-1)
    cpos = (np.arange(N_CMP) * CMP_STRIDE + CMP_BLOCK - 1).astype(f)
    angc = cpos[:, None] * inv[None]
    t = np.arange(S)
    valid = (cpos[None, :] <= t[:, None]).reshape(TB, P, N_CMP).transpose(1, 0, 2)
    causal = np.where(np.arange(P)[None, :] <= np.arange(P)[:, None], 0.0, NEG).astype(f)
    band = np.zeros((P, len(WINDOWS), TB, S), f)
    for g, w in enumerate(WINDOWS):
        m = (t[:, None] <= t[None, :]) & (t[:, None] > t[None, :] - w)
        m = m.astype(f) / np.minimum(t + 1, w).astype(f)[None, :] - np.eye(S, dtype=f)
        band[:, g] = m.reshape(TB, P, S).transpose(1, 0, 2)
    return {
        "ident": np.eye(P, dtype=f), "trig1": by_token((np.cos(ang), np.sin(ang))),
        "trig2": by_token((np.cos(ang2), np.sin(ang2))),
        "trigc": np.ascontiguousarray(np.stack([np.cos(angc), np.sin(angc)], 1)).astype(f),
        "causal": causal, "cmask": np.where(valid, 0.0, NEG).astype(f), "cvalid": valid.astype(f), "band": band,
    }


def layout(v):
    w_in, w_in2 = v["w_in"][0], v["w_in_2"][0]
    at = {"u": 0, "gp": 1024, "q": 2048, "kc": 4096, "vc": 4608, "ks": 5120, "vs": 5632, "kw": 6144, "vw": 6656,
          "gn": 7168}
    order = [("kc", 512), ("vc", 512), ("ks", 512), ("kw", 512), ("vs", 512), ("vw", 512), ("q", 2048), ("u", 1024),
             ("gp", 1024), ("gn", 2048)]
    proj = np.concatenate([w_in[:, at[n]:at[n] + k] for n, k in order], axis=1)
    gbr = np.zeros((1, P, TW), np.float32)
    gbr[0, :, :KT * 3 * NQ] = w_in[:, 9216:].reshape(KT, P, 3 * NQ).transpose(1, 0, 2).reshape(P, -1)

    def cmp_tiles(w):
        return w[0].reshape(8, 4, HD, CMP_H).transpose(0, 2, 1, 3).reshape(8, P, TW)

    pairs = np.concatenate([np.arange(0, HD, 2), np.arange(1, HD, 2)])
    qk = w_in2[:, :1280].reshape(D, 10, HD)[:, :, pairs].reshape(D, 1280)
    proj2 = np.concatenate([qk, w_in2[:, 1280:4608]], axis=1)
    merge, ffd = v["w_merge"][0], v["w_ffn_down_2"][0]

    def per_chunk(*ws):
        ts = [tiles(w).reshape(w.shape[1] // NC, -1, P, TW) for w in ws]
        return np.concatenate(ts, axis=1).reshape(-1, P, TW)

    gate_up = per_chunk(v["w_ffn_gate_2"][0], v["w_ffn_up_2"][0]).reshape(FC, 2 * T_K, P, TW)
    down = np.stack([tiles(ffd[j * NC:(j + 1) * NC]) for j in range(FC)])
    ff = np.concatenate([gate_up[1:], down[:-1]], axis=1).reshape(-1, P, TW)
    ws = np.concatenate([
        tiles(proj), gbr, cmp_tiles(v["cmp_w1_k"]), cmp_tiles(v["cmp_w1_v"]),
        per_chunk(merge[:, :D], merge[:, D:]), per_chunk(v["w_pool_out"][0], v["w_nsa_out"][0]), tiles(v["w_out"][0]),
        tiles(proj2), per_chunk(w_in2[:, 4608:6656], w_in2[:, 6656:]), per_chunk(v["w_oa_2"][0], v["w_ob_2"][0]),
        tiles(v["w_out_2"][0]), gate_up[0], ff, down[-1],
    ])
    assert len(ws) == N_TILES, (len(ws), N_TILES)
    wa = v["w_ada_2"][0].T.reshape(N_ADA, P, 2, TW).transpose(0, 2, 1, 3).reshape(2 * N_ADA, P, TW)
    rpb = v["nat_rpb_2"][0]
    tc, scol = np.arange(GRID_W)[:, None], np.arange(GRID_W)[None, :]
    start = np.clip(tc - NA_COLS // 2, 0, GRID_W - NA_COLS)
    inside = (scol >= start) & (scol < start + NA_COLS)
    rel = np.clip(scol - tc + NA_COLS - 1, 0, 2 * NA_COLS - 2)
    rows = rpb[:, NA_ROWS - ROWS:NA_ROWS + ROWS - 1]
    bias = np.where(inside, rows[:, :, rel], np.float32(NEG))
    b_merge = np.zeros((9, NC), np.float32)
    b_merge[:8] = v["b_merge"][0].reshape(2, 4, NC).transpose(1, 0, 2).reshape(8, NC)
    out = {
        "x": v["x"][0], "ws": ws, "wa": wa, "rpb": bias.transpose(0, 2, 1, 3).reshape(8, GRID_W, -1),
        "n1T": columns(v["norm_w"][0]), "n1T_2": columns(v["norm1_w_2"][0]), "n2T_2": columns(v["norm2_w_2"][0]),
        "peT": np.stack([v["cmp_pe_k"][0].T, v["cmp_pe_v"][0].T], axis=1),
        "b_adaT": columns(v["b_ada_2"][0]),
        "qkn": np.stack([v["q_norm_w_2"][0][pairs], v["k_norm_w_2"][0][pairs]]),
        "c": v["c_2"][0],
        "w2": np.stack([v[n][0].reshape(2, P, HD) for n in ("cmp_w2_k", "cmp_w2_v")]).transpose(2, 0, 1, 3),
        "mix": v["pool_mix"][0].reshape(4, 2, P, POOL_G).transpose(2, 0, 1, 3),
        "pool_scale": v["pool_scale"][0].reshape(2, NC), "b_merge": b_merge,
        "final_norm_w": v["final_norm_w"].reshape(4, NC), "final_w": v["final_w_2"].reshape(4, NC),
    }
    return {**out, **constants()}


def kernel(**inputs):
    import concourse.bacc as bacc
    from concourse.bass_utils import run_bass_kernel_spmd

    arrays = {n: np.ascontiguousarray(a) for n, a in layout({n: np.asarray(a) for n, a in inputs.items()}).items()}
    nc = bacc.Bacc("TRN2", target_bir_lowering=False, num_devices=1)
    t = {n: nc.dram_tensor(n + "_dram", a.shape, F32, kind="ExternalInput").ap() for n, a in arrays.items()}
    t["g_rows"] = nc.dram_tensor("g_rows", [2, D], F32).ap()
    t["gates"] = nc.dram_tensor("gates_spill", [2, 8, P, TB, NC], F32).ap()
    t["out"] = nc.dram_tensor("out_dram", [S, D], F32, kind="ExternalOutput").ap()
    build(nc, t)
    r = run_bass_kernel_spmd(nc, [{n + "_dram": a for n, a in arrays.items()}], core_ids=[0])
    return r.results[0]["out_dram"].reshape(1, S, D)
```
